# Optimizing a Trainium2 kernel written in Bass

```python
import functools
import jax, jax.numpy as jnp
from jax import lax
import numpy as np

D_MODEL = 1024
BATCH = 1
SEQ = 1024
DEPTH = 1
DEC_BATCH = 8
DEC_SEQ = 1
PAST_LEN = 8192
PAGE_SIZE = 128

POOL_WIDTH = D_MODEL // 2
POOL_WINDOWS = (2, 4, 8, 16)
N_POOL_GROUPS = len(POOL_WINDOWS)
POOL_GROUP_DIM = POOL_WIDTH // N_POOL_GROUPS
POOL_STATE_LEN = max(POOL_WINDOWS) - 1
N_HEADS = 8
QK_NOPE_DIM = 64
QK_ROPE_DIM = 32
QK_HEAD_DIM = QK_NOPE_DIM + QK_ROPE_DIM
V_HEAD_DIM = 64
MLA_WIDTH = N_HEADS * V_HEAD_DIM
Q_LORA_RANK = 384
KV_LORA_RANK = 256
MIX_WIDTH = POOL_WIDTH + MLA_WIDTH
IN_WIDTH = POOL_WIDTH + Q_LORA_RANK + KV_LORA_RANK + QK_ROPE_DIM
D_FF = 2816
CONV_WIDTH = 3
CONV_STATE_LEN = CONV_WIDTH - 1
ROPE_BASE = 10000.0
RMS_EPS = 1e-6
Q_BLOCK = 128

kernel_name = "hymba_pool_mla_convffn_step"

def rms_norm(x, g):
    xf = x.astype(jnp.float32)
    y = xf * lax.rsqrt(jnp.mean(xf * xf, axis=-1, keepdims=True) + RMS_EPS)
    return (y * g.astype(jnp.float32)).astype(x.dtype)

def rope_angles(pos):
    inv = ROPE_BASE ** (-jnp.arange(0, QK_ROPE_DIM, 2, dtype=jnp.float32) / QK_ROPE_DIM)
    ang = pos.astype(jnp.float32)[:, None] * inv[None, :]
    return jnp.cos(ang), jnp.sin(ang)

def apply_rope(x, cos, sin):
    x1, x2 = jnp.split(x.astype(jnp.float32), 2, axis=-1)
    return jnp.concatenate([x1 * cos - x2 * sin, x2 * cos + x1 * sin], axis=-1).astype(x.dtype)

def qk_gain(g):
    g_pe = g[QK_NOPE_DIM:]
    return jnp.concatenate([g[:QK_NOPE_DIM], g_pe, g_pe])

def mla_queries(c_q, pos, g_q_a, w_uq, g_qn):
    c_q = rms_norm(c_q, g_q_a)
    q = (c_q @ w_uq).reshape(c_q.shape[:2] + (N_HEADS, QK_HEAD_DIM))
    cos, sin = rope_angles(pos)
    q_pe = apply_rope(q[..., QK_NOPE_DIM:], cos[:, None, :], sin[:, None, :])
    q = jnp.concatenate([q[..., :QK_NOPE_DIM], q_pe], axis=-1)
    return rms_norm(q, qk_gain(g_qn))

def mla_latents(c_kv_raw, k_pe_raw, pos, g_kv_a):
    ckv = rms_norm(c_kv_raw, g_kv_a)
    cos, sin = rope_angles(pos)
    return ckv, apply_rope(k_pe_raw, cos, sin)

def mla_keys(ckv, kpe, w_uk, g_kn):
    k_nope = jnp.einsum('btc,chd->bthd', ckv, w_uk)
    k_pe = jnp.broadcast_to(kpe[:, :, None, :], k_nope.shape[:3] + (QK_ROPE_DIM,)).astype(k_nope.dtype)
    return rms_norm(jnp.concatenate([k_nope, k_pe], axis=-1), qk_gain(g_kn))

def mla_attend_prompt(q, ckv, kpe, w_uk, w_uv, g_kn):
    B, S = q.shape[:2]
    k = mla_keys(ckv, kpe, w_uk, g_kn).astype(jnp.float32)
    ckv_f = ckv.astype(jnp.float32)
    w_uv_f = w_uv.astype(jnp.float32)
    n_blocks = S // Q_BLOCK
    q_blocks = q.astype(jnp.float32).reshape(B, n_blocks, Q_BLOCK, N_HEADS, QK_HEAD_DIM).transpose(1, 0, 2, 3, 4)
    starts = jnp.arange(n_blocks, dtype=jnp.int32) * Q_BLOCK
    key_pos = jnp.arange(S, dtype=jnp.int32)
    scale = QK_HEAD_DIM ** -0.5

    def block(args):
        qb, start = args
        s = jnp.einsum('bqhd,bkhd->bhqk', qb, k) * scale
        q_pos = start + jnp.arange(Q_BLOCK, dtype=jnp.int32)
        s = jnp.where(key_pos[None, :] <= q_pos[:, None], s, -jnp.inf)
        p = jax.nn.softmax(s, axis=-1)
        ctx = jnp.einsum('bhqk,bkc->bqhc', p, ckv_f)
        return jnp.einsum('bqhc,chv->bqhv', ctx, w_uv_f)

    out = lax.map(block, (q_blocks, starts))
    return out.transpose(1, 0, 2, 3, 4).reshape(B, S, MLA_WIDTH).astype(q.dtype)

def mla_attend_sample(q, ckv_new, kpe_new, cache_ckv, cache_kpe, page_table, w_uk, w_uv, g_kn):
    B, Sq = q.shape[:2]
    qf = q.astype(jnp.float32)
    scale = QK_HEAD_DIM ** -0.5

    def update(carry, ckv_blk, kpe_blk, mask):
        m, l, acc = carry
        k = mla_keys(ckv_blk, kpe_blk, w_uk, g_kn).astype(jnp.float32)
        s = jnp.einsum('bqhd,bkhd->bhqk', qf, k) * scale
        if mask is not None:
            s = jnp.where(mask, s, -jnp.inf)
        m_new = jnp.maximum(m, jnp.max(s, axis=-1))
        alpha = jnp.exp(m - m_new)
        p = jnp.exp(s - m_new[..., None])
        l = l * alpha + jnp.sum(p, axis=-1)
        acc = acc * alpha[..., None] + jnp.einsum('bhqk,bkc->bhqc', p, ckv_blk.astype(jnp.float32))
        return (m_new, l, acc)

    init = (jnp.full((B, N_HEADS, Sq), -jnp.inf, jnp.float32),
            jnp.zeros((B, N_HEADS, Sq), jnp.float32),
            jnp.zeros((B, N_HEADS, Sq, KV_LORA_RANK), jnp.float32))

    def page_step(carry, phys):
        return update(carry, cache_ckv[phys], cache_kpe[phys], None), None

    carry, _ = lax.scan(page_step, init, page_table.T)
    causal = jnp.arange(Sq)[None, :] <= jnp.arange(Sq)[:, None]
    m, l, acc = update(carry, ckv_new, kpe_new, causal[None, None])
    ctx = acc / l[..., None]
    out = jnp.einsum('bhqc,chv->bqhv', ctx, w_uv.astype(jnp.float32))
    return out.reshape(B, Sq, MLA_WIDTH).astype(q.dtype)

def pool_mix(u, prefix, pos, w_pool, s_pool):
    B, S = u.shape[:2]
    P = POOL_STATE_LEN
    buf = jnp.concatenate([prefix.astype(u.dtype), u], axis=1)
    bf = buf.astype(jnp.float32)
    cs = jnp.concatenate([jnp.zeros((B, 1, POOL_WIDTH), jnp.float32), jnp.cumsum(bf, axis=1)], axis=1)
    end = cs[:, P + 1:P + 1 + S]
    diffs = []
    for g, w in enumerate(POOL_WINDOWS):
        ch = slice(g * POOL_GROUP_DIM, (g + 1) * POOL_GROUP_DIM)
        win = end[..., ch] - cs[:, P + 1 - w:P + 1 - w + S, ch]
        cnt = jnp.minimum(w, pos + 1).astype(jnp.float32)[None, :, None]
        diffs.append(win / cnt - bf[:, P:, ch])
    d = jnp.stack(diffs, axis=2)
    y = jnp.einsum('bsgc,gcd->bsgd', d, w_pool.astype(jnp.float32)).reshape(B, S, POOL_WIDTH)
    return (y * s_pool.astype(jnp.float32)).astype(u.dtype), buf[:, -P:]

def causal_dwconv(u, prefix, w, b):
    S = u.shape[1]
    buf = jnp.concatenate([prefix.astype(u.dtype), u], axis=1)
    y = b
    for k in range(CONV_WIDTH):
        y = y + buf[:, k:k + S] * w[k]
    return y, buf[:, -CONV_STATE_LEN:]

def trunk_layer(x, pos, pool_prefix, conv_prefix, attend, lp):
    h = rms_norm(x, lp['g_mix'])
    proj = h @ lp['w_in']
    u_pool, c_q, c_kv, k_pe = jnp.split(
        proj, [POOL_WIDTH, POOL_WIDTH + Q_LORA_RANK, POOL_WIDTH + Q_LORA_RANK + KV_LORA_RANK], axis=-1)
    pool_out, pool_state = pool_mix(u_pool, pool_prefix, pos, lp['w_pool'], lp['s_pool'])
    q = mla_queries(c_q, pos, lp['g_q_a'], lp['w_uq'], lp['g_qn'])
    ckv, kpe = mla_latents(c_kv, k_pe, pos, lp['g_kv_a'])
    attn_out = attend(q, ckv, kpe)
    g_out = lp['g_out']
    mixed = jnp.concatenate([rms_norm(pool_out, g_out[:POOL_WIDTH]),
                             rms_norm(attn_out, g_out[POOL_WIDTH:])], axis=-1)
    x = x + mixed @ lp['w_o']
    h2 = rms_norm(x, lp['g_ffn'])
    gate, conv_state = causal_dwconv(h2 @ lp['w_gate'], conv_prefix, lp['conv_w'], lp['conv_b'])
    x = x + (jax.nn.silu(gate) * (h2 @ lp['w_up'])) @ lp['w_down']
    return x, ckv, kpe, pool_state, conv_state

def setup_inputs(seed: int = 0) -> dict:
    key = jax.random.key(seed)
    ks = jax.random.split(key, 32)
    n_pages = PAST_LEN // PAGE_SIZE
    n_phys = (DEC_BATCH * n_pages * 5) // 4
    f32 = jnp.float32

    def nrm(k, shape, scale):
        return jax.random.normal(k, shape, f32) * scale

    def gain(k, shape):
        return 1.0 + 0.05 * jax.random.normal(k, shape, f32)

    perm = jax.random.permutation(ks[0], n_phys)[:DEC_BATCH * n_pages]
    return {
        "x_prompt": nrm(ks[1], (BATCH, SEQ, D_MODEL), 1.0),
        "x_sample": nrm(ks[2], (DEC_BATCH, DEC_SEQ, D_MODEL), 1.0),
        "cache_ckv": nrm(ks[3], (DEPTH, n_phys, PAGE_SIZE, KV_LORA_RANK), 1.0),
        "cache_kpe": nrm(ks[4], (DEPTH, n_phys, PAGE_SIZE, QK_ROPE_DIM), 1.0),
        "state_pool": nrm(ks[5], (DEPTH, DEC_BATCH, POOL_STATE_LEN, POOL_WIDTH), 1.0),
        "state_conv": nrm(ks[6], (DEPTH, DEC_BATCH, CONV_STATE_LEN, D_FF), 1.0),
        "page_table": perm.reshape(DEC_BATCH, n_pages).astype(jnp.int32),
        "g_mix": gain(ks[7], (DEPTH, D_MODEL)),
        "w_in": nrm(ks[8], (DEPTH, D_MODEL, IN_WIDTH), D_MODEL ** -0.5),
        "g_q_a": gain(ks[9], (DEPTH, Q_LORA_RANK)),
        "w_uq": nrm(ks[10], (DEPTH, Q_LORA_RANK, N_HEADS * QK_HEAD_DIM), Q_LORA_RANK ** -0.5),
        "g_qn": gain(ks[11], (DEPTH, QK_NOPE_DIM + QK_ROPE_DIM // 2)),
        "g_kv_a": gain(ks[12], (DEPTH, KV_LORA_RANK)),
        "w_uk": nrm(ks[13], (DEPTH, KV_LORA_RANK, N_HEADS, QK_NOPE_DIM), KV_LORA_RANK ** -0.5),
        "g_kn": gain(ks[14], (DEPTH, QK_NOPE_DIM + QK_ROPE_DIM // 2)),
        "w_uv": nrm(ks[15], (DEPTH, KV_LORA_RANK, N_HEADS, V_HEAD_DIM), KV_LORA_RANK ** -0.5),
        "w_pool": nrm(ks[16], (DEPTH, N_POOL_GROUPS, POOL_GROUP_DIM, POOL_GROUP_DIM), POOL_GROUP_DIM ** -0.5),
        "s_pool": gain(ks[17], (DEPTH, POOL_WIDTH)),
        "g_out": gain(ks[18], (DEPTH, MIX_WIDTH)),
        "w_o": nrm(ks[19], (DEPTH, MIX_WIDTH, D_MODEL), MIX_WIDTH ** -0.5),
        "g_ffn": gain(ks[20], (DEPTH, D_MODEL)),
        "w_gate": nrm(ks[21], (DEPTH, D_MODEL, D_FF), D_MODEL ** -0.5),
        "w_up": nrm(ks[22], (DEPTH, D_MODEL, D_FF), D_MODEL ** -0.5),
        "conv_w": nrm(ks[23], (DEPTH, CONV_WIDTH, D_FF), CONV_WIDTH ** -0.5),
        "conv_b": nrm(ks[24], (DEPTH, D_FF), 0.02),
        "w_down": nrm(ks[25], (DEPTH, D_FF, D_MODEL), D_FF ** -0.5),
    }

def reference(x_prompt, x_sample, cache_ckv, cache_kpe, state_pool, state_conv, page_table,
              g_mix, w_in, g_q_a, w_uq, g_qn, g_kv_a, w_uk, g_kn, w_uv, w_pool, s_pool,
              g_out, w_o, g_ffn, w_gate, w_up, conv_w, conv_b, w_down):
    B, S = x_prompt.shape[:2]
    past_len = page_table.shape[1] * PAGE_SIZE
    pos_prompt = jnp.arange(S, dtype=jnp.int32)
    pos_sample = past_len + jnp.arange(x_sample.shape[1], dtype=jnp.int32)
    yp, ys = x_prompt, x_sample
    ckv_p_l, kpe_p_l, pool_p_l, conv_p_l = [], [], [], []
    ckv_s_l, kpe_s_l, pool_s_l, conv_s_l = [], [], [], []
    for l in range(DEPTH):
        lp = {
            'g_mix': g_mix[l], 'w_in': w_in[l], 'g_q_a': g_q_a[l], 'w_uq': w_uq[l], 'g_qn': g_qn[l],
            'g_kv_a': g_kv_a[l], 'w_pool': w_pool[l], 's_pool': s_pool[l], 'g_out': g_out[l],
            'w_o': w_o[l], 'g_ffn': g_ffn[l], 'w_gate': w_gate[l], 'w_up': w_up[l],
            'conv_w': conv_w[l], 'conv_b': conv_b[l], 'w_down': w_down[l],
        }
        attend_p = functools.partial(mla_attend_prompt, w_uk=w_uk[l], w_uv=w_uv[l], g_kn=g_kn[l])
        pool0 = jnp.zeros((B, POOL_STATE_LEN, POOL_WIDTH), x_prompt.dtype)
        conv0 = jnp.zeros((B, CONV_STATE_LEN, D_FF), x_prompt.dtype)
        yp, ckv_p, kpe_p, pool_p, conv_p = trunk_layer(yp, pos_prompt, pool0, conv0, attend_p, lp)
        attend_s = functools.partial(mla_attend_sample, cache_ckv=cache_ckv[l], cache_kpe=cache_kpe[l],
                                     page_table=page_table, w_uk=w_uk[l], w_uv=w_uv[l], g_kn=g_kn[l])
        ys, ckv_s, kpe_s, pool_s, conv_s = trunk_layer(ys, pos_sample, state_pool[l], state_conv[l], attend_s, lp)
        ckv_p_l.append(ckv_p); kpe_p_l.append(kpe_p); pool_p_l.append(pool_p); conv_p_l.append(conv_p)
        ckv_s_l.append(ckv_s); kpe_s_l.append(kpe_s); pool_s_l.append(pool_s); conv_s_l.append(conv_s)
    new_ckv_prompt = jnp.stack(ckv_p_l)
    new_kpe_prompt = jnp.stack(kpe_p_l)
    new_pool_prompt = jnp.stack(pool_p_l)
    new_conv_prompt = jnp.stack(conv_p_l)
    new_ckv_sample = jnp.stack(ckv_s_l)
    new_kpe_sample = jnp.stack(kpe_s_l)
    new_pool_sample = jnp.stack(pool_s_l)
    new_conv_sample = jnp.stack(conv_s_l)
    return (yp, ys, new_ckv_prompt, new_kpe_prompt, new_pool_prompt, new_conv_prompt,
            new_ckv_sample, new_kpe_sample, new_pool_sample, new_conv_sample)


_drawn_inputs = setup_inputs


def setup_inputs(seed=0):
    import zlib

    import numpy as np

    out = dict(_drawn_inputs(seed))
    spreads = {}
    factors = {'conv_b': 7.269}
    for name, (base, spread) in spreads.items():
        noise = np.random.default_rng([zlib.crc32(name.encode()), seed]).standard_normal(out[name].shape)
        drawn = base * np.exp(spread * noise) if base else spread * noise
        out[name] = __import__('jax').numpy.asarray(drawn.astype(out[name].dtype))
    for name, factor in factors.items():
        out[name] = (out[name] * factor).astype(out[name].dtype)
    return out
```

```python
from contextlib import ExitStack

import numpy as np

import concourse.bass as bass
from concourse import mybir

F32 = mybir.dt.float32
F32R = mybir.dt.float32r
I32 = mybir.dt.int32
ALU = mybir.AluOpType
ACT = mybir.ActivationFunctionType
AX = mybir.AxisListType

P = 128
D = 1024
DC = D // P
SEQ = 1024
NB = 8
PAST = 8192
PAGE = 128
TOK = SEQ + NB
NT = SEQ // P + 1
PT = NT - 1
PW = D // 2
WINDOWS = (2, 4, 8, 16)
HIST = max(WINDOWS) - 1
NH, DN, DR, DV = 8, 64, 32, 64
DH = DN + DR
HR = DR // 2
RQ = 384
RK = 256
INW = PW + RQ + RK + DR
MIX = PW + NH * DV
FF = 2816
FC = FF // P
EPS = 1e-6
SCALE = DH ** -0.5
ROPE_BASE = 10000.0
MASKED = -3.0e38
PAGES = PAST // PAGE
F3 = TOK // 3


def row_broadcast(ap, n):
    return bass.AP(ap.tensor, ap.offset, [[0, P], [1, n]])


class Semaphores:

    def __init__(self):
        self.taken = []

    def alloc(self, nc, name):
        self.taken.append(nc.alloc_semaphore(name))
        return self.taken[-1]

    def recycle(self, nc):
        nc.clear_and_free_semaphores(self.taken)
        nc.all_engine_barrier()
        self.taken = []


SEMAPHORES = Semaphores()


class Ctx:

    def __init__(self, nc, stack, tag):
        self.nc, self.stack, self.tag = nc, stack, tag

    def sb(self, name, shape, dt=F32):
        return self.stack.enter_context(self.nc.sbuf_tensor(f"{self.tag}_{name}", shape, dt))

    def ps(self, name, shape, dt=F32):
        return self.stack.enter_context(self.nc.psum_tensor(f"{self.tag}_{name}", shape, dt))

    def sem(self, name):
        return SEMAPHORES.alloc(self.nc, f"{self.tag}_{name}")


POST = [(0, 1, 0) for _ in range(NT)]


class Steps:

    def __init__(self, eng, sem, base=None):
        self.eng, self.sem, self.n, self.base = eng, sem, 0, base

    def __call__(self, ins):
        self.n += 1
        ins.then_inc(self.sem, 1)
        self.wait(self.n)

    def mark(self, ins):
        self.n += 1
        ins.then_inc(self.sem, 1)
        return self.n

    def wait(self, n):
        self.eng.wait_ge(self.sem, n if self.base is None else self.base + n)


def newton_rsqrt(dve, step, out, mean, guess, tmp):
    step(dve.tensor_tensor(tmp, guess, guess, ALU.mult))
    step(dve.tensor_tensor(tmp, tmp, mean, ALU.mult))
    step(dve.tensor_scalar(tmp, tmp, -0.5, 1.5, ALU.mult, ALU.add))
    return dve.tensor_tensor(out, tmp, guess, ALU.mult)


def project_in(nc, io, keep):
    WB = 4
    with ExitStack() as stack:
        c = Ctx(nc, stack, "in")
        w_more = c.sb("w_raw", [P, WB - 1, INW])
        w_raw = [w_more[:, n, :] for n in range(WB - 1)] + [keep.ctx[:].rearrange("p b c -> p (b c)")[:, 0:INW]]
        w_hi = c.sb("w_hi", [P, DC, INW], F32R)
        w_lo = c.sb("w_lo", [P, DC, INW], F32R)
        eps = c.sb("eps", [P, 1])
        x, xn = (keep.room[:, n * D:(n + 2) * D].rearrange("p (b d) -> p b d", b=2) for n in (0, 2))
        junk, gain = keep.room[:, 4 * D:5 * D], keep.room[:, 5 * D:6 * D]
        hT_hi = c.sb("hT_hi", [P, 2, DC, P], F32R)
        hT_lo = c.sb("hT_lo", [P, 2, DC, P], F32R)
        u_nat = keep.room[:, 6 * D:7 * D].rearrange("p (b n) -> p b n", b=2)
        gain_q, gain_kv = keep.room[:, 7 * D:7 * D + RQ], keep.room[:, 7 * D + RQ:7 * D + RQ + RK]
        cq_nat = c.sb("cq_nat", [P, RQ])
        ckv_nat = c.sb("ckv_nat", [P, 2, RK])
        kpe_raw = c.sb("kpe_raw", [P, DR])
        rot = c.sb("rot", [P, 4, HR])
        ssx = c.sb("ssx", [P, NT])
        lnx = c.sb("lnx", [P, NT])
        gx = c.sb("gx", [P, NT])
        tx = c.sb("tx", [P, NT])
        rx = c.sb("rx", [P, NT])
        ssl = c.sb("ssl", [P, NT, 2])
        lnl = c.sb("lnl", [P, NT, 2])
        gl = c.sb("gl", [P, NT, 2])
        tl = c.sb("tl", [P, NT, 2])
        rl = c.sb("rl", [P, NT, 2])
        tr = c.ps("tr", [P, 2, 512])
        out = c.ps("out", [P, 2, 3, 512])

        w_in = [c.sem(f"w_in{n}") for n in range(WB)]
        const_in = c.sem("const_in")
        gain_in = c.sem("gain_in")
        pages_in, ident_in, w_kv_in = c.sem("pages_in"), c.sem("ident_in"), c.sem("w_kv_in")
        x_in = [c.sem(f"x_in{n}") for n in range(2)]
        eps_set = c.sem("eps_set")
        pad_set = c.sem("pad_set")
        w_hi_done, w_lo_done = c.sem("w_hi_done"), c.sem("w_lo_done")
        ssx_done, gx_done, xn_done = c.sem("ssx_done"), c.sem("gx_done"), c.sem("xn_done")
        act_step, dve_step, pool_step = c.sem("act_step"), c.sem("dve_step"), c.sem("pool_step")
        x_turned, u_turned, q_turned, kv_turned = (c.sem("x_turned"), c.sem("u_turned"), c.sem("q_turned"),
                                                   c.sem("kv_turned"))
        hi_done, lo_done = c.sem("hi_done"), c.sem("lo_done")
        u_kept, q_kept, kv_kept = c.sem("u_kept"), c.sem("q_kept"), c.sem("kv_kept")
        projected = c.sem("projected")
        squared, gl_done = c.sem("squared"), c.sem("gl_done")
        u_out = c.sem("u_out")
        cq_normed, ckv_normed, kpe_out = c.sem("cq_normed"), c.sem("ckv_normed"), c.sem("kpe_out")
        roped = c.sem("roped")
        stored_kv = [c.sem(f"stored_kv{n}") for n in range(2)]
        stored_u, stored_pe, copied = c.sem("stored_u"), c.sem("stored_pe"), c.sem("copied")
        x_rows = io["x_prompt"].rearrange("b (t p) d -> (b t) p d", p=P)
        block = stack.enter_context(nc.Block())

        @block.sync
        def _(sp):
            def load_x(i):
                if i >= 2:
                    sp.wait_ge(xn_done, i - 1)
                if i < PT:
                    sp.dma_start(x[:, i % 2, :], x_rows[i]).then_inc(x_in[i % 2], 16)
                else:
                    sp.wait_ge(pad_set, 1)
                    sp.dma_start(x[0:NB, i % 2, :], io["x_sample"].rearrange("b s d -> (b s) d"))\
                      .then_inc(x_in[i % 2], 16)

            load_x(0)
            sp.dma_start(gain, row_broadcast(io["g_mix"], D)).then_inc(gain_in, 16)
            sp.dma_start(keep.ident[:], io["ident"]).then_inc(ident_in, 16)
            for k in range(WB):
                sp.dma_start(w_raw[k], io["w_in"][0, k * P:(k + 1) * P, :]).then_inc(w_in[k], 16)
                if k == 1:
                    load_x(1)
            for k in range(WB, DC):
                sp.wait_ge(w_lo_done, k - WB + 1)
                sp.dma_start(w_raw[k % WB], io["w_in"][0, k * P:(k + 1) * P, :]).then_inc(w_in[k % WB], 16)
            for t, name in ((keep.w_uk, "w_uk"), (keep.w_uv, "w_uv")):
                sp.dma_start(t[:], io[name][0].rearrange("(c p) h d -> p c (h d)", p=P)).then_inc(w_kv_in, 16)
            sp.dma_start(io["new_pool_sample"][0, :, 0:HIST - 1, :], io["state_pool"][0, :, 1:HIST, :])\
              .then_inc(copied, 16)
            sp.dma_start(io["new_conv_sample"][0, :, 0, :], io["state_conv"][0, :, 1, :]).then_inc(copied, 16)
            for i in range(NT):
                if i + 2 < NT:
                    load_x(i + 2)
                rows = P if i < PT else NB
                dst = (lambda name, n: io[f"new_{name}_prompt"][0, 0, i * P:(i + 1) * P, :] if i < PT
                       else io[f"new_{name}_sample"][0, :, 0, :])
                sp.wait_ge(ckv_normed, i + 1)
                sp.dma_start(dst("ckv", RK), ckv_nat[0:rows, i % 2, :]).then_inc(stored_kv[i % 2], 16)
                if i >= PT - 1:
                    sp.wait_ge(u_out, i + 1)
                    if i < PT:
                        sp.dma_start(io["new_pool_prompt"][0, 0, :, :], u_nat[P - HIST:P, i % 2, :])\
                          .then_inc(stored_u, 16)
                    else:
                        sp.dma_start(io["new_pool_sample"][0, :, HIST - 1, :], u_nat[0:NB, i % 2, :])\
                          .then_inc(stored_u, 16)
                sp.wait_ge(roped, i + 1)
                sp.dma_start(dst("kpe", DR), keep.kpe[0:rows, i, :]).then_inc(stored_pe, 16)
            sp.wait_ge(stored_kv[0], 16 * ((NT + 1) // 2))
            sp.wait_ge(stored_kv[1], 16 * (NT // 2))
            sp.wait_ge(stored_pe, 16 * NT)
            sp.wait_ge(stored_u, 32)
            sp.wait_ge(copied, 32)
            sp.wait_ge(w_kv_in, 32)

        @block.scalar
        def _(act):
            step = Steps(act, act_step)
            act.preload_act_table_set("natural_log_exp_and_others")

            def stats(i):
                act.wait_ge(x_in[i % 2], 16 * (i // 2 + 1))
                if i == PT:
                    act.wait_ge(pad_set, 1)
                step(nc.scalar.activation(junk, x[:, i % 2, :], ACT.Square, accum_out=ssx[:, i:i + 1]))
                step(nc.scalar.activation(lnx[:, i:i + 1], ssx[:, i:i + 1], ACT.Ln, bias=eps[:], scale=1.0 / D))
                nc.scalar.activation(gx[:, i:i + 1], lnx[:, i:i + 1], ACT.Exp, scale=-0.5).then_inc(gx_done, 1)

            def hi(i):
                for half in range(2):
                    act.wait_ge(x_turned, 2 * i + half + 1)
                    if i >= 2:
                        act.wait_ge(projected, i - 1)
                    nc.scalar.activation(hT_hi[:, i % 2, 4 * half:4 * half + 4, :],
                                         tr[:, half, :].rearrange("p (c t) -> p c t", t=P),
                                         ACT.Copy).then_inc(hi_done, 1)

            def latents(i):
                act.wait_ge(projected, i + 1)
                b = i % 2
                step(nc.scalar.activation(junk[:, 0:RQ], out[:, b, 1, 0:RQ], ACT.Square, accum_out=ssl[:, i, 0:1]))
                step(nc.scalar.activation(junk[:, 0:RK], out[:, b, 2, 0:RK], ACT.Square, accum_out=ssl[:, i, 1:2]))
                step(nc.scalar.activation(lnl[:, i, 0:1], ssl[:, i, 0:1], ACT.Ln, bias=eps[:], scale=1.0 / RQ))
                step(nc.scalar.activation(lnl[:, i, 1:2], ssl[:, i, 1:2], ACT.Ln, bias=eps[:], scale=1.0 / RK))
                nc.scalar.activation(gl[:, i, :], lnl[:, i, :], ACT.Exp, scale=-0.5).then_inc(gl_done, 1)
                if i >= 2:
                    act.wait_ge(u_turned, i - 1)
                    if i >= PT + 1:
                        act.wait_ge(stored_u, 16)
                nc.scalar.activation(u_nat[:, b, :], out[:, b, 0, 0:PW], ACT.Copy).then_inc(u_out, 1)

            def kept(i):
                cols = slice(i * P, (i + 1) * P)
                act.wait_ge(u_turned, i + 1)
                bu, bq, bk = POST[i]
                if i < PT:
                    nc.scalar.activation(keep.uT[:, :, HIST + i * P:HIST + (i + 1) * P],
                                         tr[:, bu, :].rearrange("p (g t) -> p g t", t=P), ACT.Copy).then_inc(u_kept, 1)
                else:
                    nc.scalar.activation(keep.usT[:, :, :, HIST],
                                         tr[:, bu, :].rearrange("p (g t) -> p g t", t=P)[:, :, 0:NB],
                                         ACT.Copy).then_inc(u_kept, 1)
                act.wait_ge(q_turned, i + 1)
                nc.scalar.activation(keep.cqT[:, :, cols], tr[:, bq, 0:RQ].rearrange("p (g t) -> p g t", t=P),
                                     ACT.Copy).then_inc(q_kept, 1)
                act.wait_ge(kv_turned, i + 1)
                nc.scalar.activation(keep.ckvT[:, :, cols], tr[:, bk, 0:RK].rearrange("p (g t) -> p g t", t=P),
                                     ACT.Copy).then_inc(kv_kept, 1)

            act.wait_ge(eps_set, 1)
            stats(0)
            stats(1)
            for k in range(DC):
                act.wait_ge(w_in[k % WB], 16 * (k // WB + 1))
                nc.scalar.activation(w_hi[:, k, :], w_raw[k % WB], ACT.Copy).then_inc(w_hi_done, 1)
                if k == 1:
                    hi(0)
            for i in range(NT):
                if i + 1 < NT:
                    hi(i + 1)
                if i + 2 < NT:
                    stats(i + 2)
                if i >= 1:
                    kept(i - 1)
                latents(i)
            kept(NT - 1)

        @block.tensor
        def _(pe):
            pe.wait_ge(ident_in, 16)

            def x_unit(i, half):
                if half == 0:
                    pe.wait_ge(xn_done, i + 1)
                free(half)
                for j in range(4):
                    k = 4 * half + j
                    last = nc.tensor.transpose(tr[:, half, j * P:(j + 1) * P], xn[:, i % 2, k * P:(k + 1) * P],
                                               keep.ident[:])
                last.then_inc(x_turned, 1)
                user[half] = (lo_done, 2 * i + half + 1)

            user = [None, None]

            def free(bank):
                if user[bank]:
                    pe.wait_ge(*user[bank])

            def post_unit(i, which):
                bank = POST[i][which]
                ready, turned, src, n, kept_sem = (
                    (u_out, u_turned, u_nat[:, i % 2, :], 4, u_kept),
                    (cq_normed, q_turned, cq_nat[:, :], 3, q_kept),
                    (ckv_normed, kv_turned, ckv_nat[:, i % 2, :], 2, kv_kept))[which]
                pe.wait_ge(ready, i + 1)
                free(bank)
                for j in range(n):
                    last = nc.tensor.transpose(tr[:, bank, j * P:(j + 1) * P], src[:, j * P:(j + 1) * P],
                                               keep.ident[:])
                last.then_inc(turned, 1)
                user[bank] = (kept_sem, i + 1)

            x_unit(0, 0)
            x_unit(0, 1)
            for i in range(NT):
                b = i % 2
                if i >= 2:
                    pe.wait_ge(kpe_out, i - 1)
                    pe.wait_ge(u_out, i - 1)
                for k in range(DC):
                    if i == 0:
                        pe.wait_ge(w_lo_done, k + 1)
                    pe.wait_ge(lo_done, 2 * i + k // 4 + 1)
                    for n, (h, w) in enumerate(((hT_hi, w_hi), (hT_hi, w_lo), (hT_lo, w_hi))):
                        for g, (lo, hi) in enumerate(((0, PW), (PW, PW + RQ), (PW + RQ, INW))):
                            last = nc.tensor.matmul(out[:, b, g, 0:hi - lo], h[:, b, k, :], w[:, k, lo:hi],
                                                    start=(k == 0 and n == 0), stop=(k == DC - 1 and n == 2))
                    if i + 1 < NT and k < 2:
                        x_unit(i + 1, k)
                    if i >= 1 and k in (4, 5, 6):
                        post_unit(i - 1, k - 4)
                last.then_inc(projected, 1)
            for which in range(3):
                post_unit(NT - 1, which)

        @block.vector
        def _(dve):
            step = Steps(dve, dve_step)
            nc.vector.memset(eps[:], EPS).then_inc(eps_set, 1)
            nc.vector.memset(keep.uT[:, :, 0:HIST], 0.0)
            dve.wait_ge(gain_in, 16)

            def norm_x(i):
                n = slice(i, i + 1)
                dve.wait_ge(gx_done, i + 1)
                step(nc.vector.tensor_scalar(tx[:, n], ssx[:, n], 1.0 / D, EPS, ALU.mult, ALU.add))
                step(newton_rsqrt(nc.vector, step, rx[:, n], tx[:, n], gx[:, n], lnx[:, n]))
                if i >= 2:
                    dve.wait_ge(x_turned, 2 * i - 2)
                nc.vector.scalar_tensor_tensor(out=xn[:, i % 2, :], in0=x[:, i % 2, :], scalar=rx[:, n], in1=gain,
                                               op0=ALU.mult, op1=ALU.mult).then_inc(xn_done, 1)
                if i == PT - 2:
                    dve.wait_ge(xn_done, i + 1)
                    nc.vector.memset(x[:, 0, :], 0.0).then_inc(pad_set, 1)

            def lo(i):
                for half in range(2):
                    dve.wait_ge(hi_done, 2 * i + half + 1)
                    nc.vector.tensor_tensor(hT_lo[:, i % 2, 4 * half:4 * half + 4, :],
                                            tr[:, half, :].rearrange("p (c t) -> p c t", t=P),
                                            hT_hi[:, i % 2, 4 * half:4 * half + 4, :].bitcast(F32),
                                            ALU.subtract).then_inc(lo_done, 1)

            def latents(i):
                b = i % 2
                dve.wait_ge(u_out, i + 1)
                step(nc.vector.tensor_scalar(tl[:, i, 0:1], ssl[:, i, 0:1], 1.0 / RQ, EPS, ALU.mult, ALU.add))
                step(nc.vector.tensor_scalar(tl[:, i, 1:2], ssl[:, i, 1:2], 1.0 / RK, EPS, ALU.mult, ALU.add))
                step(newton_rsqrt(nc.vector, step, rl[:, i, :], tl[:, i, :], gl[:, i, :], lnl[:, i, :]))
                if i >= 1:
                    dve.wait_ge(q_turned, i)
                nc.vector.scalar_tensor_tensor(out=cq_nat[:], in0=out[:, b, 1, 0:RQ], scalar=rl[:, i, 0:1],
                                               in1=gain_q, op0=ALU.mult, op1=ALU.mult).then_inc(cq_normed, 1)
                if i >= 2:
                    dve.wait_ge(kv_turned, i - 1)
                    dve.wait_ge(stored_kv[b], 16 * (i // 2))
                nc.vector.scalar_tensor_tensor(out=ckv_nat[:, b, :], in0=out[:, b, 2, 0:RK], scalar=rl[:, i, 1:2],
                                               in1=gain_kv, op0=ALU.mult, op1=ALU.mult).then_inc(ckv_normed, 1)
                dve.wait_ge(cq_normed, i + 1)
                if i >= 1:
                    dve.wait_ge(roped, i)
                nc.vector.tensor_copy(kpe_raw[:], out[:, b, 2, RK:RK + DR]).then_inc(kpe_out, 1)

            for k in range(DC):
                if k == 0:
                    norm_x(0)
                if k == 2:
                    lo(0)
                if k == 4:
                    norm_x(1)
                dve.wait_ge(w_hi_done, k + 1)
                dve.wait_ge(w_in[k % WB], 16 * (k // WB + 1))
                nc.vector.tensor_tensor(w_lo[:, k, :], w_raw[k % WB], w_hi[:, k, :].bitcast(F32),
                                        ALU.subtract).then_inc(w_lo_done, 1)
            dve.wait_ge(const_in, 16 * 4)
            for i in range(NT):
                if i + 1 < NT:
                    lo(i + 1)
                if i + 2 < NT:
                    norm_x(i + 2)
                latents(i)

        @block.gpsimd
        def _(pool):
            step = Steps(pool, pool_step)
            for t, n, ap in ((gain_q, RQ, "g_q_a"), (gain_kv, RK, "g_kv_a")):
                pool.dma_start(t, row_broadcast(io[ap], n)).then_inc(const_in, 16)
            pool.dma_start(keep.cos[:], io["rope_cos"]).then_inc(const_in, 16)
            pool.dma_start(keep.sin[:], io["rope_sin"]).then_inc(const_in, 16)
            table = io["page_table"]
            with nc.allow_non_contiguous_dma(reason="512 page numbers, once"):
                for a in range(8):
                    pool.dma_start(keep.pages[16 * a:16 * a + 16, :],
                                 bass.AP(table.tensor, table.offset + a, [[0, 16], [8, PAST // CHUNK * NB]]))\
                      .then_inc(pages_in, 16)
                pool.dma_start(keep.g_out[:], io["g_out"][0].rearrange("(c p) -> p c", p=P)).then_inc(pages_in, 16)
            for t, name in ((keep.sub_row, "sub_row"), (keep.fold, "fold"), (keep.own, "own")):
                pool.dma_start(t[:], io[name]).then_inc(pages_in, 16)
            nc.gpsimd.memset(keep.ones[:], 1.0)
            pool.wait_ge(const_in, 16 * 4)
            for i in range(NT):
                pool.wait_ge(kpe_out, i + 1)
                a, b_ = kpe_raw[:, 0:HR], kpe_raw[:, HR:DR]
                cos, sin = keep.cos[:, i, :], keep.sin[:, i, :]
                nc.gpsimd.tensor_tensor(rot[:, 0, :], a, cos, ALU.mult)
                nc.gpsimd.tensor_tensor(rot[:, 1, :], b_, sin, ALU.mult)
                nc.gpsimd.tensor_tensor(rot[:, 2, :], b_, cos, ALU.mult)
                step(nc.gpsimd.tensor_tensor(rot[:, 3, :], a, sin, ALU.mult))
                step(nc.gpsimd.tensor_tensor(keep.kpe[:, i, 0:HR], rot[:, 0, :], rot[:, 1, :], ALU.subtract))
                nc.gpsimd.tensor_tensor(keep.kpe[:, i, HR:DR], rot[:, 2, :], rot[:, 3, :], ALU.add).then_inc(roped, 1)
            pool.wait_ge(pages_in, 16 * 12)


def make_heads(nc, io, keep):
    with ExitStack() as stack:
        c = Ctx(nc, stack, "hd")
        w_uq = c.sb("w_uq", [P, RQ // P, NH * DH])
        w_uk, w_uv = keep.w_uk, keep.w_uv
        w_pool = c.sb("w_pool", [P, 4, P])
        s_pool = c.sb("s_pool", [P, 4])
        g_col = c.sb("g_col", [DH, 2])
        gqk_col = c.sb("gqk_col", [DH, 1])
        g_row = c.sb("g_row", [P, 2, DH])
        counts = c.sb("counts", [P, 4, 16])
        sq_q = c.sb("sq_q", [P, NH * DH])
        sq_k = c.sb("sq_k", [P, NH * DN])
        sq_e = c.sb("sq_e", [P, DR])
        kpe_ss = c.sb("kpe_ss", [P, NT])
        ss = c.sb("ss", [P, 2, NH])
        mean = c.sb("mean", [P, 2 * NH])
        log = c.sb("log", [P, 2 * NH])
        guess = c.sb("guess", [P, 2 * NH])
        rs = c.sb("rs", [P, 2 * NH])
        spare, q_size = keep.ctx[:].rearrange("p b c -> p (b c)"), 2 * NH * DH
        q_nat = spare[:, 0:q_size].rearrange("p (n h d) -> p n h d", n=2, h=NH)
        rot = spare[:, q_size:q_size + 4 * NH * HR].rearrange("p (n h d) -> p n h d", n=4, h=NH)
        k_nat = c.sb("k_nat", [P, 2, NH, DH])
        run = keep.mixT[:, 1:4, :].rearrange("p g t -> p (g t)")[:, 0:2 * (HIST + SEQ)].rearrange("p (n t) -> p n t", n=2)
        state = keep.mixT[0:NB * HIST, 0, 0:PW]
        dT = keep.mixT[:, 4:8, :]
        s_sum = c.sb("s_sum", [P, 4, NB])
        Q = c.ps("Q", [P, 2, 2, 512])
        K = c.ps("K", [P, 2, 512])
        T = c.ps("T", [P, 2, 512])

        consts, w_uq_in = c.sem("consts"), c.sem("w_uq_in")
        projected, units, unit_out = c.sem("projected"), c.sem("units"), c.sem("unit_out")
        squared, summed, guessed = c.sem("squared"), c.sem("summed"), c.sem("guessed")
        q_scaled, k_ready, rotated = c.sem("q_scaled"), c.sem("k_ready"), c.sem("rotated")
        act_step, dve_step, pool_step = c.sem("act_step"), c.sem("dve_step"), c.sem("pool_step")
        gains = c.sem("gains")
        state_turned, state_kept = c.sem("state_turned"), c.sem("state_kept")
        windows, sample_d = c.sem("windows"), c.sem("sample_d")
        y_made, y_kept = c.sem("y_made"), c.sem("y_kept")
        NCONST = 10
        UNITS = ([(i, u) for i in range(PT) for u in range(5)] + [("y", g, j) for g in range(4) for j in range(2)]
                 + [(PT, 3), (PT, 4)] + [("y", g, 2) for g in range(4)])
        number = {unit: n for n, unit in enumerate(UNITS)}
        block = stack.enter_context(nc.Block())

        @block.sync
        def _(sp):
            col = lambda ap, a, n: ap[0, a:a + n].rearrange("(p o) -> p o", o=1)
            sp.dma_start(w_uq[:], io["w_uq"][0].rearrange("(c p) n -> p c n", p=P)).then_inc(w_uq_in, 16)
            sp.dma_start(state, io["state_pool"][0].rearrange("b r c -> (b r) c")).then_inc(consts, 16)
            sp.dma_start(w_pool[:], io["w_pool"][0].rearrange("g c d -> c g d")).then_inc(consts, 16)
            sp.dma_start(counts[:], io["counts"]).then_inc(consts, 16)
            with nc.allow_non_contiguous_dma(reason="gains as columns, a few hundred values"):
                sp.dma_start(s_pool[:], io["s_pool"][0].rearrange("(g p) -> p g", p=P)).then_inc(consts, 16)
                for j, name in enumerate(("g_qn", "g_kn")):
                    sp.dma_start(g_col[0:DN + HR, j:j + 1], col(io[name], 0, DN + HR)).then_inc(consts, 16)
                    sp.dma_start(g_col[DN + HR:DH, j:j + 1], col(io[name], DN, HR)).then_inc(consts, 16)
            for j, name in enumerate(("g_qn", "g_kn")):
                sp.dma_start(g_row[:, j, 0:DN + HR], row_broadcast(io[name], DN + HR)).then_inc(consts, 16)

        @block.tensor
        def _(pe):
            def project(i):
                cols = slice(i * P, (i + 1) * P)
                if i >= 2:
                    pe.wait_ge(q_scaled, i - 1)
                    pe.wait_ge(k_ready, i - 1)
                for k in range(2):
                    nc.tensor.matmul(K[:, i % 2, :], keep.ckvT[:, k, cols], w_uk[:, k, :],
                                     start=(k == 0), stop=(k == 1))
                if i == 0:
                    pe.wait_ge(w_uq_in, 16)
                for k in range(RQ // P):
                    for g in range(2):
                        last = nc.tensor.matmul(Q[:, i % 2, g, 0:4 * DH], keep.cqT[:, k, cols],
                                                w_uq[:, k, g * 4 * DH:(g + 1) * 4 * DH], start=(k == 0), stop=(k == 2))
                last.then_inc(projected, 1)

            def bank(n):
                if n >= 2:
                    pe.wait_ge(unit_out, n - 1)
                return T[:, n % 2, :]

            def turn(i):
                cols = slice(i * P, (i + 1) * P)
                for u in range(5):
                    if (i, u) not in number:
                        continue
                    t = bank(number[i, u])
                    if u == 0:
                        for k in range(2):
                            last = nc.tensor.matmul(t[:, :], keep.ckvT[:, k, cols], w_uv[:, k, :],
                                                    start=(k == 0), stop=(k == 1))
                        last.then_inc(units, 1)
                        continue
                    src = (k_nat if u < 3 else q_nat)[:, i % 2]
                    if u == 1:
                        pe.wait_ge(k_ready, i + 1)
                    if u == 3:
                        pe.wait_ge(rotated, i + 1)
                    for j in range(4):
                        last = nc.tensor.transpose(t[0:DH, j * P:(j + 1) * P], src[:, 4 * ((u - 1) % 2) + j, :],
                                                   keep.ident[:])
                    last.then_inc(units, 1)

            project(0)
            pe.wait_ge(consts, 16 * NCONST)
            for g in range(4):
                last = nc.tensor.transpose(K[:, 1, g * P:g * P + NB * HIST], state[:, g * P:(g + 1) * P],
                                           keep.ident[0:NB * HIST, 0:NB * HIST])
            last.then_inc(state_turned, 1)
            for i in range(1, NT):
                if i == 1:
                    pe.wait_ge(state_kept, 1)
                project(i)
                turn(i - 1)

            def pooled(g, j):
                pe.wait_ge(windows, g + 1)
                nc.tensor.matmul(bank(number["y", g, j])[:, 0:F3], w_pool[:, g, :], dT[:, g, j * F3:(j + 1) * F3],
                                 start=True, stop=True).then_inc(units, 1)

            for g in range(4):
                for j in range(2):
                    pooled(g, j)
            turn(NT - 1)
            pe.wait_ge(sample_d, 1)
            for g in range(4):
                pooled(g, 2)

        @block.scalar
        def _(act):
            step = Steps(act, act_step)
            act.wait_ge(consts, 16 * NCONST)
            act.wait_ge(state_turned, 1)
            nc.scalar.activation(keep.usT[:, :, :, 0:HIST],
                                 K[:, 1, :].rearrange("p (g n) -> p g n", n=P)[:, :, 0:NB * HIST]
                                 .rearrange("p g (b r) -> p g b r", r=HIST), ACT.Copy).then_inc(state_kept, 1)

            def squares(i):
                act.wait_ge(projected, i + 1)
                if i >= 1:
                    act.wait_ge(summed, i)
                nc.scalar.activation(sq_q[:].rearrange("p (g n) -> p g n", g=2), Q[:, i % 2, :, 0:4 * DH], ACT.Square)
                nc.scalar.activation(sq_k[:], K[:, i % 2, :], ACT.Square)
                if i >= 1:
                    act.wait_ge(squared, i)
                nc.scalar.activation(sq_e[:], keep.kpe[:, i, :], ACT.Square,
                                     accum_out=kpe_ss[:, i:i + 1]).then_inc(squared, 1)

            def guesses(i):
                act.wait_ge(summed, i + 1)
                if i >= 1:
                    act.wait_ge(k_ready, i)
                step(nc.scalar.activation(log[:], mean[:], ACT.Ln))
                nc.scalar.activation(guess[:], log[:], ACT.Exp, scale=-0.5).then_inc(guessed, 1)

            def keep_units(i, us):
                for u in us:
                    if (i, u) not in number:
                        continue
                    n = number[i, u]
                    act.wait_ge(units, n + 1)
                    t = T[:, n % 2, :]
                    heads = t[0:DH, :].rearrange("p (h t) -> p h t", t=P)
                    hs = slice(4 * ((u - 1) % 2), 4 * ((u - 1) % 2) + 4)
                    cols = slice(i * P, (i + 1) * P) if i < PT else slice(SEQ, TOK)
                    m = P if i < PT else NB
                    if u == 0:
                        nc.scalar.activation(keep.v[:, i, :], t[:, :], ACT.Copy).then_inc(unit_out, 1)
                    elif u < 3:
                        nc.scalar.activation(keep.kT[:, hs, cols], heads[:, :, 0:m], ACT.Copy).then_inc(unit_out, 1)
                    else:
                        if i == 0 and u == 3:
                            act.wait_ge(gains, 1)
                        dst = keep.qT[:, hs, cols] if i < PT else keep.q_new[:, hs, :]
                        nc.scalar.activation(dst, heads[:, :, 0:m], ACT.Copy,
                                             scale=gqk_col[:]).then_inc(unit_out, 1)

            for i in range(NT):
                squares(i)
                if i >= 1:
                    keep_units(i - 1, (0, 1, 2))
                guesses(i)
                if i >= 1:
                    keep_units(i - 1, (3, 4))

            def keep_pooled(g, j):
                n = number["y", g, j]
                act.wait_ge(units, n + 1)
                if j == 0 and g >= 1:
                    act.wait_ge(windows, 4)
                nc.scalar.activation(keep.mixT[:, g, j * F3:(j + 1) * F3], T[:, n % 2, 0:F3], ACT.Copy,
                                     scale=s_pool[:, g:g + 1]).then_inc(unit_out, 1)

            for g in range(4):
                for j in range(2):
                    keep_pooled(g, j)
            keep_units(NT - 1, range(5))
            for g in range(4):
                keep_pooled(g, 2)

        @block.vector
        def _(dve):
            step = Steps(dve, dve_step)
            dve.wait_ge(consts, 16 * NCONST)
            nc.vector.tensor_scalar(keep.index[:], keep.pages[:], float(PAGE // 8), keep.sub_row[:], ALU.mult, ALU.add)
            nc.vector.scalar_tensor_tensor(out=gqk_col[:], in0=g_col[:, 0:1], scalar=SCALE, in1=g_col[:, 1:2],
                                           op0=ALU.mult, op1=ALU.mult).then_inc(gains, 1)
            step(nc.vector.tensor_copy(g_row[:, :, DN + HR:DH], g_row[:, :, DN:DN + HR]))
            step(nc.vector.scalar_tensor_tensor(out=g_row[:, 0, :], in0=g_row[:, 0, :], scalar=SCALE,
                                                in1=g_row[:, 1, :], op0=ALU.mult, op1=ALU.mult))

            def sums(i):
                dve.wait_ge(squared, i + 1)
                step(nc.vector.tensor_reduce(ss[:, 0, :], sq_q[:].rearrange("p (h d) -> p h d", d=DH), AX.X, ALU.add))
                step(nc.vector.tensor_reduce(ss[:, 1, :], sq_k[:].rearrange("p (h d) -> p h d", d=DN), AX.X, ALU.add))
                step(nc.vector.tensor_scalar(ss[:, 1, :], ss[:, 1, :], kpe_ss[:, i:i + 1], None, ALU.add))
                nc.vector.tensor_scalar(mean[:], ss[:].rearrange("p a h -> p (a h)"), 1.0 / DH, EPS,
                                        ALU.mult, ALU.add).then_inc(summed, 1)

            def scale_heads(i):
                b = i % 2
                dve.wait_ge(guessed, i + 1)
                dve.wait_ge(summed, i + 1)
                step(newton_rsqrt(nc.vector, step, rs[:], mean[:], guess[:], log[:]))
                if i >= 2:
                    dve.wait_ge(units, 5 * (i - 1))
                rq = rs[:, 0:NH].unsqueeze(2).to_broadcast([P, NH, DH])
                rk = rs[:, NH:2 * NH].unsqueeze(2)
                for g in range(2):
                    last = nc.vector.tensor_tensor(q_nat[:, b, 4 * g:4 * g + 4, :],
                                                   Q[:, b, g, 0:4 * DH].rearrange("p (h d) -> p h d", d=DH),
                                                   rq[:, 4 * g:4 * g + 4, :], ALU.mult)
                last.then_inc(q_scaled, 1)
                nc.vector.tensor_tensor(k_nat[:, b, :, 0:DN], K[:, b, :].rearrange("p (h d) -> p h d", d=DN),
                                        rk.to_broadcast([P, NH, DN]), ALU.mult)
                nc.vector.tensor_tensor(k_nat[:, b, :, DN:DH], keep.kpe[:, i:i + 1, :].to_broadcast([P, NH, DR]),
                                        rk.to_broadcast([P, NH, DR]), ALU.mult).then_inc(k_ready, 1)

            def sample_windows():
                dve.wait_ge(state_kept, 1)
                for g, w in enumerate(WINDOWS):
                    last = nc.vector.tensor_reduce(s_sum[:, g, :], keep.usT[:, g, :, HIST + 1 - w:HIST + 1], AX.X, ALU.add)
                step(last)
                for g, w in enumerate(WINDOWS):
                    last = nc.vector.scalar_tensor_tensor(out=dT[:, g, SEQ:TOK], in0=s_sum[:, g, :], scalar=1.0 / w,
                                                          in1=keep.usT[:, g, :, HIST], op0=ALU.mult, op1=ALU.subtract)
                last.then_inc(sample_d, 1)

            for i in range(NT):
                sums(i)
                scale_heads(i)
                if i == 0:
                    sample_windows()
            b = PT % 2
            prod = sq_q[0:NB, :].rearrange("p (h d) -> p h d", h=NH)
            dve.wait_ge(rotated, NT)
            dve.wait_ge(k_ready, NT)
            dve.wait_ge(units, 5 * PT)
            step(nc.vector.tensor_tensor(keep.q_s[:], q_nat[0:NB, b], g_row[0:NB, 0:1, :].to_broadcast([NB, NH, DH]),
                                         ALU.mult))
            step(nc.vector.tensor_tensor(prod, keep.q_s[:], k_nat[0:NB, b], ALU.mult))
            step(nc.vector.tensor_reduce(keep.s_own[:], prod, AX.X, ALU.add))

        @block.gpsimd
        def _(pool):
            step = Steps(pool, pool_step)
            pool.wait_ge(consts, 16 * NCONST)

            def rotate(i):
                pool.wait_ge(q_scaled, i + 1)
                a, b_ = q_nat[:, i % 2, :, DN:DN + HR], q_nat[:, i % 2, :, DN + HR:DH]
                cos = keep.cos[:, i:i + 1, :].to_broadcast([P, NH, HR])
                sin = keep.sin[:, i:i + 1, :].to_broadcast([P, NH, HR])
                nc.gpsimd.tensor_tensor(rot[:, 0], a, cos, ALU.mult)
                nc.gpsimd.tensor_tensor(rot[:, 1], b_, sin, ALU.mult)
                nc.gpsimd.tensor_tensor(rot[:, 2], b_, cos, ALU.mult)
                step(nc.gpsimd.tensor_tensor(rot[:, 3], a, sin, ALU.mult))
                nc.gpsimd.tensor_tensor(a, rot[:, 0], rot[:, 1], ALU.subtract)
                nc.gpsimd.tensor_tensor(b_, rot[:, 2], rot[:, 3], ALU.add).then_inc(rotated, 1)
                pool.wait_ge(rotated, i + 1)

            def window(g):
                src = keep.uT[:, g, :]
                for j in range(g + 1):
                    w, dst = 1 << j, run[:, j % 2, :]
                    done = 2 * w - 1
                    step(nc.gpsimd.tensor_tensor(dst[:, done:], src[:, done:], src[:, done - w:HIST + SEQ - w], ALU.add))
                    src = dst
                means = run[:, (g + 1) % 2, HIST:]
                step(nc.gpsimd.tensor_scalar(means, src[:, HIST:], 1.0 / WINDOWS[g], 1.0, ALU.mult, ALU.mult))
                step(nc.gpsimd.tensor_tensor(means[:, 0:16], src[:, HIST:HIST + 16], counts[:, g, :], ALU.mult))
                nc.gpsimd.tensor_tensor(dT[:, g, 0:SEQ], means, keep.uT[:, g, HIST:], ALU.subtract)\
                  .then_inc(windows, 1)
                pool.wait_ge(windows, g + 1)

            for i in range(NT):
                rotate(i)
                if i % 2 == 0 and i // 2 < 4:
                    window(i // 2)


def attend_prompt(nc, io, keep):
    with ExitStack() as stack:
        c = Ctx(nc, stack, "at")
        causal = c.sb("causal", [P, P])
        probs = c.sb("probs", [P, 2, SEQ])
        pT = c.sb("pT", [P, 2, 2, SEQ])
        nmax = c.sb("nmax", [P, 2])
        total = c.sb("total", [P, 2])
        inv = c.sb("inv", [P, 2])
        S = c.ps("S", [P, 2, SEQ])
        T = c.ps("T", [P, 2, 512])
        O = c.ps("O", [P, 2, 512])
        mask_in = c.sem("mask_in")
        scored, masked, maxed, exped, normed = (c.sem(n) for n in ("scored", "masked", "maxed", "exped", "normed"))
        inverted = c.sem("inverted")
        turned, kept = c.sem("turned"), c.sem("kept")
        mixed, out_kept = c.sem("mixed"), c.sem("out_kept")
        stored = c.sem("stored")
        items = [(hp, i if hp % 2 == 0 else PT - 1 - i, e) for hp in range(NH // 2) for i in range(PT)
                 for e in range(2)]
        units = [(n, a, min(4, i + 1 - a)) for n, (hp, i, e) in enumerate(items) for a in range(0, i + 1, 4)]
        first_unit = [next(u for u, (m, _, _) in enumerate(units) if m == n) for n in range(len(items))] + [len(units)]
        block = stack.enter_context(nc.Block())

        @block.sync
        def _(sp):
            sp.dma_start(causal[:], io["causal"]).then_inc(mask_in, 16)
            sp.dma_start(keep.mixed_dram[:, 0:4, :], keep.mixT[:, 0:4, :]).then_inc(stored, 16)
            for hp in range(NH // 2):
                sp.wait_ge(out_kept, PT * (hp + 1))
                sp.dma_start(keep.mixed_dram[:, 4 + hp, 0:SEQ], keep.mixT[:, 4 + hp, 0:SEQ]).then_inc(stored, 16)
            sp.wait_ge(stored, 16 * (1 + NH // 2))

        @block.tensor
        def _(pe):
            def score(n):
                hp, i, e = items[n]
                if n >= 2:
                    pe.wait_ge(exped, n - 1)
                h = 2 * hp + e
                for a in range(0, (i + 1) * P, 512):
                    z = min((i + 1) * P, a + 512)
                    last = nc.tensor.matmul(S[:, n % 2, a:z], keep.qT[:, h, i * P:(i + 1) * P], keep.kT[:, h, a:z],
                                            start=True, stop=True)
                last.then_inc(scored, 1)

            def turn(n):
                for u in range(first_unit[n], first_unit[n + 1]):
                    _, a, m = units[u]
                    pe.wait_ge(normed, u + 1)
                    if u >= 2:
                        pe.wait_ge(kept, u - 1)
                    for j in range(m):
                        last = nc.tensor.transpose(T[:, u % 2, j * P:(j + 1) * P],
                                                   probs[:, n % 2, (a + j) * P:(a + j + 1) * P], keep.ident[:])
                    last.then_inc(turned, 1)

            def mix(s):
                hp, i, _ = items[2 * s]
                pe.wait_ge(kept, first_unit[2 * s + 2])
                if s >= 2:
                    pe.wait_ge(out_kept, s - 1)
                for k in range(i + 1):
                    for e in range(2):
                        h = 2 * hp + e
                        last = nc.tensor.matmul(O[e * DV:(e + 1) * DV, s % 2, 0:P], keep.v[:, k, h * DV:(h + 1) * DV],
                                                pT[:, s % 2, e, k * P:(k + 1) * P], start=(k == 0), stop=(k == i))
                last.then_inc(mixed, 1)

            score(0)
            score(1)
            for n in range(len(items)):
                if n + 2 < len(items):
                    score(n + 2)
                if n % 2 == 0 and n >= 2:
                    mix(n // 2 - 1)
                turn(n)
            mix(len(items) // 2 - 1)

        @block.vector
        def _(dve):
            dve.wait_ge(mask_in, 16)

            def peak(n):
                _, i, _ = items[n]
                dve.wait_ge(scored, n + 1)
                diag = S[:, n % 2, i * P:(i + 1) * P]
                nc.vector.tensor_tensor(diag, diag, causal[:], ALU.add).then_inc(masked, 1)
                dve.wait_ge(masked, n + 1)
                if n >= 2:
                    dve.wait_ge(exped, n - 1)
                nc.vector.tensor_reduce(nmax[:, n % 2:n % 2 + 1], S[:, n % 2, 0:(i + 1) * P], AX.X, ALU.max,
                                        negate=True).then_inc(maxed, 1)

            def norm(n):
                _, i, _ = items[n]
                dve.wait_ge(exped, n + 1)
                b = slice(n % 2, n % 2 + 1)
                nc.vector.reciprocal(inv[:, b], total[:, b]).then_inc(inverted, 1)
                dve.wait_ge(inverted, n + 1)
                for u in range(first_unit[n], first_unit[n + 1]):
                    _, a, m = units[u]
                    p = probs[:, n % 2, a * P:(a + m) * P]
                    nc.vector.tensor_scalar(p, p, inv[:, b], None, ALU.mult).then_inc(normed, 1)

            peak(0)
            for n in range(len(items)):
                if n + 1 < len(items):
                    peak(n + 1)
                norm(n)

        def keep_unit(u):
            n, a, m = units[u]
            return (pT[:, (n // 2) % 2, n % 2, a * P:(a + m) * P], T[:, u % 2, 0:m * P])

        @block.scalar
        def _(act):
            def exp(n):
                _, i, _ = items[n]
                act.wait_ge(maxed, n + 1)
                if n >= 2:
                    act.wait_ge(turned, first_unit[n - 1])
                nc.scalar.activation(probs[:, n % 2, 0:(i + 1) * P], S[:, n % 2, 0:(i + 1) * P], ACT.Exp,
                                     bias=nmax[:, n % 2:n % 2 + 1], accum_out=total[:, n % 2:n % 2 + 1])\
                  .then_inc(exped, 1)

            def keep_p(n):
                if n % 2 == 0 and n >= 4:
                    act.wait_ge(mixed, n // 2 - 1)
                for u in range(first_unit[n], first_unit[n + 1]):
                    act.wait_ge(turned, u + 1)
                    dst, src = keep_unit(u)
                    nc.scalar.activation(dst, src, ACT.Copy).then_inc(kept, 1)

            def keep_out(s):
                hp, i, _ = items[2 * s]
                act.wait_ge(mixed, s + 1)
                nc.scalar.activation(keep.mixT[:, 4 + hp, i * P:(i + 1) * P], O[:, s % 2, 0:P], ACT.Copy)\
                  .then_inc(out_kept, 1)

            exp(0)
            for n in range(len(items)):
                if n + 1 < len(items):
                    exp(n + 1)
                keep_p(n)
                if n % 2 == 1 and n >= 3:
                    keep_out(n // 2 - 1)
            keep_out(len(items) // 2 - 1)


CHUNK = P * 8
CHUNKS = PAST // CHUNK
TILES = PAST // P
PAIRS = TILES // 2
HALF = NH // 2 * DN + NH // 2


def gather(nc, io, keep, par, b):
    for n in range(CHUNKS):
        s = par * CHUNKS + n
        at = bass.IndirectOffsetOnAxis(ap=keep.index[:, b * CHUNKS + n:b * CHUNKS + n + 1], axis=0)
        for dst, name in ((keep.kpe_slots, "cache_kpe"), (keep.lat, "cache_ckv")):
            rows = io[name][0].rearrange("n (s k) c -> (n s) (k c)", k=8)
            nc.gpsimd.indirect_dma_start(dst[:, s, :], None, rows, at).then_inc(keep.slot_in[s], 16)


def attend_cache(nc, io, keep):
    with ExitStack() as stack:
        c = Ctx(nc, stack, "ca")
        lat, kpe, slot_in = keep.lat, keep.kpe_slots, keep.slot_in
        w_hi = c.sb("w_hi", [P, 2, 2, HALF], F32R)
        w_lo = c.sb("w_lo", [P, 2, 2, HALF], F32R)
        hi = c.sb("hi", [P, 2, 2, 2, P], F32R)
        lo = c.sb("lo", [P, 2, 2, 2, P], F32R)
        sq = c.sb("sq", [P, 2, 2, 4 * DN])
        kpeT = c.sb("kpeT", [P, 2, P])
        kpe_sq = c.sb("kpe_sq", [P, 8, DR])
        q_pe = c.sb("q_pe", [P, P])
        raw = c.sb("raw", [P, 2, TILES + 1, NH])
        rot = c.sb("rot", [P, 2, TILES, NH])
        ss = c.sb("ss", [P, 2, TILES, NH])
        kss = c.sb("kss", [P, 2, TILES])
        mean = c.sb("mean", [P, TILES, NH])
        guess, tmp = (keep.w_uv[:, n, :].rearrange("p (t h) -> p t h", h=NH) for n in range(2))
        top = c.sb("top", [P, NH])
        top_all = c.sb("top_all", [P, NH])
        probs = c.sb("probs", [P, TILES + 1, NH])
        KK = c.ps("KK", [P, 2, 2, 512])
        TT = c.ps("TT", [P, 2, 512])
        KP = c.ps("KP", [P, 512])
        CT = c.ps("CT", [P, 512])

        w_set, q_set, cleared = c.sem("w_set"), c.sem("q_set"), c.sem("cleared")
        turned, hi_done, lo_done = c.sem("turned"), c.sem("hi_done"), c.sem("lo_done")
        keyed, squared, summed, scored = c.sem("keyed"), c.sem("squared"), c.sem("summed"), c.sem("scored")
        pe_turned, pe_kept, pe_scored, pe_out = (c.sem("pe_turned"), c.sem("pe_kept"), c.sem("pe_scored"),
                                                 c.sem("pe_out"))
        averaged, guessed, maxed, reduced = c.sem("averaged"), c.sem("guessed"), c.sem("maxed"), c.sem("reduced")
        shifted, probs_done, weighted, ctx_out = (c.sem("shifted"), c.sem("probs_done"), c.sem("weighted"),
                                                  c.sem("ctx_out"))
        totalled = c.sem("totalled")
        complete, pool_step = c.sem("complete"), c.sem("pool_step")
        act_step, kpe_squared, pe_summed = (c.sem("act_step"), c.sem("kpe_squared"),
                                                      c.sem("pe_summed"))
        consts, zeroed = c.sem("consts"), c.sem("zeroed")
        w_turned, w_kept = c.sem("w_turned"), c.sem("w_kept")
        absorbed, qa_hi_done, rep_done, rep_turned = (c.sem(n) for n in ("absorbed", "qa_hi_done", "rep_done",
                                                                        "rep_turned"))
        prepared, dve_step = c.sem("prepared"), c.sem("dve_step")
        w_ukT = [t[0:DN].rearrange("p n t h -> p (n t h)").rearrange("p (h k) -> p h k", h=NH) for t in (rot, ss)]
        rep = raw[0:NB].rearrange("p n t h -> p (n t h)")[:, 0:NH * 4 * DR].rearrange("p (h s d) -> p h s d", h=NH, s=4)
        mine, off = (mean[0:NB].rearrange("p t h -> p (t h)")[:, n * NB * NH:(n + 1) * NB * NH]
                     .rearrange("p (b h) -> p b h", h=NH) for n in range(2))
        W = KK[:].rearrange("p t a n -> p (t a) n")
        A = TT[:, 0, 0:2 * NH * NB].rearrange("p (c h b) -> p c h b", c=2, h=NH)
        B = TT[:, 1, 0:NH * NB].rearrange("p (h b) -> p h b", h=NH)
        block = stack.enter_context(nc.Block())

        @block.sync
        def _(sp):
            sp.wait_ge(zeroed, 1)
            sp.dma_start(keep.ckv_s[0:NB, :], io["new_ckv_sample"][0, :, 0, :]).then_inc(consts, 16)

        PARTS = ((0, TILES * 3 // 4), (TILES * 3 // 4, TILES))

        def sequences(eng, body, last=None):
            body(0, 0, 0)
            with eng.Fori(0, (NB - 2) // 2) as j:
                body(1, j * 2 + 1, j)
                body(0, j * 2 + 2, j + 1)
            body(1, NB - 1, NB // 2 - 1)

        @block.gpsimd
        def _(pool):
            def tail(b):
                par = b % 2
                if b >= 1:
                    pool.wait_ge(shifted, b)
                for n, (a, z) in enumerate(PARTS if b == NB - 1 else ((0, TILES),)):
                    pool.wait_ge(summed, b * TILES + z)
                    pool.wait_ge(pe_summed, b * CHUNKS + z // 8)
                    step(nc.gpsimd.tensor_tensor(mean[:, a:z], ss[:, par, a:z], kss[:, par, a:z].unsqueeze(2)
                                                 .to_broadcast([P, z - a, NH]), ALU.add))
                    nc.gpsimd.tensor_scalar(mean[:, a:z], mean[:, a:z], 1.0 / DH, EPS, ALU.mult, ALU.add)\
                      .then_inc(averaged, 1)
                    pool.wait_ge(scored, b * TILES + z)
                    pool.wait_ge(pe_out, b * CHUNKS + z // 8)
                    step(nc.gpsimd.tensor_tensor(raw[:, par, a:z], raw[:, par, a:z], rot[:, par, a:z], ALU.add))
                    pool.wait_ge(averaged, b + 1 + n)
                    pool.wait_ge(guessed, b + 1 + n)
                    step(newton_rsqrt(nc.gpsimd, step, guess[:, a:z], mean[:, a:z], guess[:, a:z], tmp[:, a:z]))
                    step(nc.gpsimd.tensor_tensor(raw[:, par, a:z], raw[:, par, a:z], guess[:, a:z], ALU.mult))
                nc.gpsimd.tensor_copy(raw[:, par, TILES, :], keep.s_new[:, b, :]).then_inc(complete, 1)
                pool.wait_ge(maxed, b + 1)
                nc.gpsimd.partition_all_reduce(top_all[:], top[:], P, bass.bass_isa.ReduceOp.max).then_inc(reduced, 1)
                pool.wait_ge(reduced, b + 1)
                nc.gpsimd.tensor_tensor(raw[:, par], raw[:, par], top_all[:].unsqueeze(1)
                                        .to_broadcast([P, TILES + 1, NH]), ALU.subtract).then_inc(shifted, 1)

            step = Steps(pool, pool_step)
            gather(nc, io, keep, 0, 0)
            gather(nc, io, keep, 1, 1)
            for b in range(NB):
                tail(b)
                if b + 2 < NB:
                    pool.wait_ge(weighted, b + 1)
                    gather(nc, io, keep, b % 2, b + 2)

        @block.tensor
        def _(pe):
            def chunk_in(par, r, n):
                pe.wait_ge(slot_in[par * CHUNKS + n], r * 32 + 32)

            def turn(par, b, r, n):
                if n % 4 == 0:
                    chunk_in(par, r, n // 4)
                if n >= 2 or not isinstance(b, int) or b > 0:
                    pe.wait_ge(lo_done, b * PAIRS + n - 1)
                for t in range(2):
                    for ck in range(2):
                        k = (2 * n + t) % 8
                        src = lat[:, par * CHUNKS + n // 4, k * RK + ck * P:k * RK + (ck + 1) * P]
                        last = nc.tensor.transpose(TT[:, n % 2, (2 * t + ck) * P:(2 * t + ck + 1) * P], src,
                                                   keep.ident[:])
                last.then_inc(turned, 1)

            def keys(b, n):
                pe.wait_ge(lo_done, b * PAIRS + n + 1)
                for t in range(2):
                    if n >= 1 or not isinstance(b, int) or b > 0:
                        pe.wait_ge(scored, b * TILES + 2 * n + t - 1)
                    terms = [(x, w, ck) for ck in range(2) for x, w in ((hi, w_hi), (hi, w_lo), (lo, w_hi))]
                    for m, (x, w, ck) in enumerate(terms):
                        for half in range(2):
                            last = nc.tensor.matmul(KK[:, t, half, 0:HALF], x[:, n % 2, t, ck, :], w[:, ck, half, :],
                                                    start=(m == 0), stop=(m == 5))
                    last.then_inc(keyed, 1)

            def turn_rotary(par, b, n):
                if n >= 1 or not isinstance(b, int) or b > 0:
                    pe.wait_ge(pe_out, b * CHUNKS + n)
                for g in range(2):
                    last = nc.tensor.transpose(KP[:, g * P:(g + 1) * P], kpe[:, par * CHUNKS + n, g * P:(g + 1) * P],
                                               keep.ident[:])
                last.then_inc(pe_turned, 1)

            def rotary(b, n):
                pe.wait_ge(pe_kept, b * CHUNKS + n + 1)
                for g in range(2):
                    last = nc.tensor.matmul(KP[:, (2 + g) * P:(3 + g) * P], kpeT[:, g, :], q_pe[:], start=True, stop=True)
                last.then_inc(pe_scored, 1)

            def weigh(par, b):
                pe.wait_ge(probs_done, b + 1)
                if not isinstance(b, int) or b > 0:
                    pe.wait_ge(ctx_out, b)
                for t in range(TILES + 1):
                    q = t % 4
                    v = lat[:, par * CHUNKS + t // 8, (t % 8) * RK:(t % 8 + 1) * RK] if t < TILES else keep.ckv_s[:]
                    last = nc.tensor.matmul(CT[q * 32:q * 32 + NH, 0:RK], probs[:, t, :], v, start=(t < 4),
                                            stop=(t >= TILES - 3))
                last.then_inc(weighted, 1)

            def sequence(par, b, r):
                first, final = (isinstance(b, int) and b == n for n in (0, NB - 1))
                if first:
                    turn(par, b, r, 0)
                for n in range(PAIRS):
                    if n == 0:
                        pe.wait_ge(q_set, b + 1)
                    if n % 4 == 0:
                        turn_rotary(par, b, n // 4)
                    if n == 14 and not first:
                        weigh(1 - par, b - 1)
                    if n + 1 < PAIRS:
                        turn(par, b, r, n + 1)
                    elif not final:
                        turn(1 - par, b + 1, r + par, 0)
                    keys(b, n)
                    if n % 4 == 1:
                        rotary(b, n // 4)

            for n in range(4):
                for j in range(4):
                    h, ck = divmod(4 * n + j, 2)
                    last = nc.tensor.transpose(W[0:DN, n, j * P:(j + 1) * P], keep.w_uk[:, ck, h * DN:(h + 1) * DN],
                                               keep.ident[:])
                last.then_inc(w_turned, 1)
            pe.wait_ge(rep_done, 1)
            for h in range(NH):
                last = nc.tensor.transpose(B[:, h, :], rep[:, h].rearrange("b s d -> b (s d)"),
                                           keep.ident[0:NB, 0:NB])
            last.then_inc(rep_turned, 1)
            pe.wait_ge(w_kept, 2)
            for ck in range(2):
                for h in range(NH):
                    last = nc.tensor.matmul(A[:, ck, h, :], w_ukT[ck][:, h, :], keep.q_new[0:DN, h, :],
                                            start=True, stop=True)
            last.then_inc(absorbed, 1)
            pe.wait_ge(cleared, 1)
            pe.wait_ge(prepared, 1)
            pe.wait_ge(consts, 16)
            sequences(pe, sequence)
            weigh(1, NB - 1)

        @block.scalar
        def _(act):
            def sequence(par, b, r):
                later = not isinstance(b, int) or b > 0
                for n in range(PAIRS):
                    act.wait_ge(turned, b * PAIRS + n + 1)
                    if n >= 2 or later:
                        act.wait_ge(keyed, b * TILES + 2 * n - 2)
                    nc.scalar.activation(hi[:, n % 2], TT[:, n % 2, :].rearrange("p (t c k) -> p t c k", t=2, c=2),
                                         ACT.Copy).then_inc(hi_done, 1)
                    if n == 3 and later:
                        guess_norms(b - 1)
                    if n == 27 and isinstance(b, int) and b == NB - 1:
                        guess_norms(b, 0, *PARTS[0])
                    if n == 12 and later:
                        exp(1 - par, b - 1)
                    if n >= 1:
                        squares(b, n - 1)
                    elif later:
                        squares(b - 1, PAIRS - 1)
                    if n % 4 == 0:
                        rotary_turned(par, b, n // 4)

            def rotary_turned(par, b, n):
                act.wait_ge(pe_turned, b * CHUNKS + n + 1)
                if n >= 1 or not isinstance(b, int) or b > 0:
                    act.wait_ge(pe_scored, b * CHUNKS + n)
                nc.scalar.activation(kpeT[:].rearrange("p g k -> p (g k)"), KP[:, 0:2 * P], ACT.Copy).then_inc(pe_kept, 1)
                if n >= 1 or not isinstance(b, int) or b > 0:
                    act.wait_ge(pe_summed, b * CHUNKS + n)
                nc.scalar.activation(kpe_sq[:].rearrange("p k d -> p (k d)"), kpe[:, par * CHUNKS + n, :], ACT.Square)\
                  .then_inc(kpe_squared, 1)

            def squares(b, n):
                for t in range(2):
                    act.wait_ge(keyed, b * TILES + 2 * n + t + 1)
                    if n >= 1 or not isinstance(b, int) or b > 0:
                        act.wait_ge(summed, b * TILES + 2 * n + t - 1)
                    nc.scalar.activation(sq[:, t], KK[:, t, :, 0:4 * DN], ACT.Square).then_inc(squared, 1)

            def guess_norms(b, part=0, a=0, z=TILES):
                act.wait_ge(averaged, b + 1 + part)
                nc.scalar.activation(tmp[:, a:z], mean[:, a:z], ACT.Ln).then_inc(act_step, 1)
                act.wait_ge(act_step, b + 1 + part)
                nc.scalar.activation(guess[:, a:z], tmp[:, a:z], ACT.Exp, scale=-0.5).then_inc(guessed, 1)

            def exp(par, b):
                act.wait_ge(shifted, b + 1)
                if not isinstance(b, int):
                    act.wait_ge(weighted, b)
                elif b > 0:
                    act.wait_ge(weighted, b)
                nc.scalar.activation(probs[:], raw[:, par], ACT.Exp).then_inc(probs_done, 1)

            act.wait_ge(w_turned, 4)
            for ck in range(2):
                nc.scalar.activation(w_ukT[ck].rearrange("p (n a) k -> p n a k", a=2),
                                     W[0:DN].rearrange("p n (a c k) -> p n a c k", a=2, c=2)[:, :, :, ck, :],
                                     ACT.Copy).then_inc(w_kept, 1)
            for ck in range(2):
                last = nc.scalar.activation(w_hi[:, ck, :, 0:4 * DN], keep.w_uk[:, ck, :].rearrange("p (a n) -> p a n", a=2),
                                            ACT.Copy)
            last.then_inc(w_set, 1)
            act.wait_ge(absorbed, 1)
            for ck in range(2):
                last = nc.scalar.activation(keep.qa_hi[:, ck, :, :], A[:, ck].rearrange("p h b -> p b h"), ACT.Copy)
            last.then_inc(qa_hi_done, 1)
            sequences(act, sequence)
            squares(NB - 1, PAIRS - 1)
            guess_norms(NB - 1, 1, *PARTS[1])
            exp(1, NB - 1)

        @block.vector
        def _(dve):
            def queries(par, b):
                if not isinstance(b, int) or b > 0:
                    dve.wait_ge(keyed, b * TILES)
                    dve.wait_ge(pe_scored, b * CHUNKS)
                for dst, src in ((w_hi, keep.qa_hi), (w_lo, keep.qa_lo)):
                    for ck in range(2):
                        nc.vector.tensor_scalar(dst[:, ck, :, 4 * DN:HALF],
                                                src[:, ck, bass.ds(b, 1), :].bitcast(F32)
                                                .rearrange("p o (a h) -> p (o a) h", a=2), 1.0, None, ALU.mult)
                nc.vector.tensor_scalar(q_pe[:, 0:4 * NH], keep.q_pe[:, bass.ds(b, 1)].rearrange("p o s h -> p (o s h)"),
                                        1.0, None, ALU.mult)\
                  .then_inc(q_set, 1)

            def sequence(par, b, r):
                later = not isinstance(b, int) or b > 0
                for n in range(PAIRS):
                    dve.wait_ge(hi_done, b * PAIRS + n + 1)
                    if n >= 2 or later:
                        dve.wait_ge(keyed, b * TILES + 2 * n - 2)
                    nc.vector.tensor_tensor(lo[:, n % 2], TT[:, n % 2, :].rearrange("p (t c k) -> p t c k", t=2, c=2),
                                            hi[:, n % 2].bitcast(F32), ALU.subtract).then_inc(lo_done, 1)
                    if n == 0:
                        if later:
                            sums(1 - par, b - 1, PAIRS - 1, (0,))
                        queries(par, b)
                        if later:
                            sums(1 - par, b - 1, PAIRS - 1, (1,))
                    if n >= 1:
                        sums(par, b, n - 1)
                    if n % 4 == 3:
                        rotary_scores(par, b, n // 4)
                    if later:
                        tail(1 - par, b - 1, n)

            def sums(par, b, n, tiles=(0, 1)):
                for t in tiles:
                    dve.wait_ge(squared, b * TILES + 2 * n + t + 1)
                    nc.vector.tensor_reduce(ss[:, par, 2 * n + t, :], sq[:, t].rearrange("p a (h d) -> p (a h) d", d=DN),
                                            AX.X, ALU.add).then_inc(summed, 1)
                    nc.vector.tensor_copy(raw[:, par, 2 * n + t, :].rearrange("p (a h) -> p a h", a=2),
                                          KK[:, t, :, 4 * DN:HALF]).then_inc(scored, 1)

            def rotary_scores(par, b, n):
                dve.wait_ge(pe_scored, b * CHUNKS + n + 1)
                nc.vector.tensor_copy(rot[:, par, 8 * n:8 * n + 8, :].rearrange("p (g s) h -> p g (s h)", g=2),
                                      KP[:, 2 * P:4 * P].rearrange("p (g k) -> p g k", g=2)[:, :, 0:4 * NH])\
                  .then_inc(pe_out, 1)
                dve.wait_ge(kpe_squared, b * CHUNKS + n + 1)
                nc.vector.tensor_reduce(kss[:, par, 8 * n:8 * n + 8], kpe_sq[:], AX.X, ALU.add)\
                  .then_inc(pe_summed, 1)

            def tail(par, b, n):
                if n == 10:
                    dve.wait_ge(complete, b + 1)
                    nc.vector.tensor_reduce(top[:], raw[:, par].rearrange("p t h -> p h t"), AX.X, ALU.max)\
                      .then_inc(maxed, 1)
                elif n == 15:
                    dve.wait_ge(probs_done, b + 1)
                    nc.vector.tensor_reduce(keep.total[:, bass.ds(b, 1), :].rearrange("p o h -> p (o h)"),
                                            probs[:].rearrange("p t h -> p h t"), AX.X, ALU.add)\
                      .then_inc(totalled, 1)
                elif n == 20:
                    dve.wait_ge(weighted, b + 1)
                    nc.vector.tensor_scalar(keep.ctx[:, bass.ds(b, 1), :].rearrange("p o c -> p (o c)"), CT[:, 0:RK],
                                            1.0, None, ALU.mult).then_inc(ctx_out, 1)

            step = Steps(dve, dve_step)
            nc.vector.memset(keep.ckv_s[:], 0.0).then_inc(zeroed, 1)
            nc.vector.memset(keep.q_pe[:], 0.0)
            nc.vector.memset(keep.s_new[:], MASKED)
            nc.vector.tensor_copy(rep, keep.q_s[:, :, DN:DH].unsqueeze(2).to_broadcast([NB, NH, 4, DR]))\
              .then_inc(rep_done, 1)
            step(nc.vector.tensor_scalar(off, keep.own[:], 1.0, -MASKED, ALU.subtract, ALU.mult))
            step(nc.vector.tensor_tensor(mine, keep.own[:], keep.s_own[:].unsqueeze(1).to_broadcast([NB, NB, NH]),
                                         ALU.mult))
            nc.vector.tensor_tensor(keep.s_new[0:NB], mine, off, ALU.add)
            nc.vector.memset(CT[:], 0.0)
            nc.vector.memset(q_pe[:], 0.0).then_inc(cleared, 1)
            dve.wait_ge(cleared, 1)
            dve.wait_ge(w_set, 1)
            for ck in range(2):
                nc.vector.tensor_tensor(w_lo[:, ck, :, 0:4 * DN], keep.w_uk[:, ck, :].rearrange("p (a n) -> p a n", a=2),
                                        w_hi[:, ck, :, 0:4 * DN].bitcast(F32), ALU.subtract)
            dve.wait_ge(rep_turned, 1)
            for s in range(4):
                rows = slice(DR * s, DR * (s + 1))
                last = nc.vector.tensor_copy(keep.q_pe[rows, :, s, :], B[rows].rearrange("p h b -> p b h"))
            dve.wait_ge(qa_hi_done, 1)
            for ck in range(2):
                last = nc.vector.tensor_tensor(keep.qa_lo[:, ck, :, :], A[:, ck].rearrange("p h b -> p b h"),
                                               keep.qa_hi[:, ck, :, :].bitcast(F32), ALU.subtract)
            last.then_inc(prepared, 1)
            dve.wait_ge(prepared, 1)
            sequences(dve, sequence)
            sums(1, NB - 1, PAIRS - 1)
            for n in range(PAIRS):
                tail(1, NB - 1, n)


def merge(nc, io, keep):
    with ExitStack() as stack:
        c = Ctx(nc, stack, "mg")
        w_hi = c.sb("w_hi", [P, DC, D], F32R)
        w_lo = c.sb("w_lo", [P, DC, D], F32R)
        g_ffn = c.sb("g_ffn", [P, D])
        eps = c.sb("eps", [P, 1])
        m = c.sb("m", [P, 2, DC, P])
        x = c.sb("x", [P, 2, D])
        m_hi = c.sb("m_hi", [P, 2, DC, P], F32R)
        m_lo = c.sb("m_lo", [P, 2, DC, P], F32R)
        sq = c.sb("sq", [P, 2, 4, P])
        x1 = c.sb("x1", [P, 2, D])
        w_more = c.sb("w_raw", [P, 2, D])
        w_raw = [w_more[:, 0, :], w_more[:, 1, :], x1[:, 0, :], x1[:, 1, :]]
        WB = len(w_raw)
        h2 = c.sb("h2", [P, D])
        junk = h2
        ctxT = c.sb("ctxT", [P, 2, NH, NB])
        total = c.sb("total", [NB, NH])
        own = c.sb("own", [NB, NB, NH])
        inv = c.sb("inv", [NB, NH])
        out = m[0:NB, 1].rearrange("p c t -> p (c t)")[:, 0:NH * DV]
        outT = c.sb("outT", [P, 4, NB])
        mean = c.sb("mean", [P, 3])
        ssx = c.sb("ssx", [P, NT])
        log = c.sb("log", [P, 3])
        guess = c.sb("guess", [P, 3])
        r_mix = c.sb("r_mix", [P, 2, 2])
        r_x1 = c.sb("r_x1", [P, 1])
        OUT = c.ps("OUT", [P, 2, 2, 512])
        SS = c.ps("SS", [P, 2, P])
        T = c.ps("T", [P, 2, 512])
        F = T[:, 0, 0:P].rearrange("p (b c h) -> p b c h", b=NB, c=2)
        L, OT, O = SS[:, 0, 0:NB * NH], OUT[:, 1, 1, 0:4 * NB], T[0:NB, 1, :]
        w_uv_in = c.sem("w_uv_in")
        folded, fold_out, sums_made = c.sem("folded"), c.sem("fold_out"), c.sem("sums_made")
        head_out, head_normed, head_turned, head_kept, head_stored = (
            c.sem("head_out"), c.sem("head_normed"), c.sem("head_turned"), c.sem("head_kept"), c.sem("head_stored"))
        w_in = [c.sem(f"w_in{n}") for n in range(WB)]
        m_in = [c.sem(f"m_in{n}") for n in range(2)]
        x_in = [c.sem(f"x_in{n}") for n in range(2)]
        consts, pad_set = c.sem("consts"), c.sem("pad_set")
        w_hi_done, w_lo_done = c.sem("w_hi_done"), c.sem("w_lo_done")
        squared, summed, averaged, guessed = c.sem("squared"), c.sem("summed"), c.sem("averaged"), c.sem("guessed")
        m_hi_done, m_lo_done, half_done, x1_half = (c.sem("m_hi_done"), c.sem("m_lo_done"), c.sem("half_done"),
                                                    c.sem("x1_half"))
        x_guessed, normed = c.sem("x_guessed"), c.sem("normed")
        turned, hi_done, lo_done = c.sem("turned"), c.sem("hi_done"), c.sem("lo_done")
        stored = [c.sem(f"stored{n}") for n in range(2)]
        act_step, dve_step, pool_step = c.sem("act_step"), c.sem("dve_step"), c.sem("pool_step")
        chunks_added = c.sem("chunks_added")
        x_rows = io["x_prompt"].rearrange("b (t p) d -> (b t) p d", p=P)
        block = stack.enter_context(nc.Block())

        @block.sync
        def _(sp):
            def load(i):
                b = i % 2
                if i >= 2:
                    sp.wait_ge(m_lo_done, i - 1)
                    sp.wait_ge(x1_half, 2 * i - 2)
                if i == 1:
                    sp.wait_ge(head_turned, 1)
                if i < PT:
                    sp.dma_start(m[:, b], keep.mixed_dram[:, :, i * P:(i + 1) * P]).then_inc(m_in[b], 16)
                    sp.dma_start(x[:, b, :], x_rows[i]).then_inc(x_in[b], 16)
                else:
                    sp.wait_ge(pad_set, 2)
                    sp.wait_ge(head_stored, 16)
                    with nc.allow_non_contiguous_dma(reason="eight columns of decode tokens"):
                        sp.dma_start(m[:, b, :, 0:NB], keep.mixed_dram[:, :, SEQ:TOK]).then_inc(m_in[b], 16)
                    sp.dma_start(x[0:NB, b, :], io["x_sample"].rearrange("b s d -> (b s) d")).then_inc(x_in[b], 16)

            for k in range(DC):
                if k >= WB:
                    sp.wait_ge(w_lo_done, k - WB + 1)
                sp.dma_start(w_raw[k % WB], io["w_o"][0, k * P:(k + 1) * P, :]).then_inc(w_in[k % WB], 16)
                if k == 0:
                    sp.dma_start(keep.w_uv[:], io["w_uv"][0].rearrange("(c p) h d -> p c (h d)", p=P)).then_inc(w_uv_in, 16)
                if k == 1:
                    load(0)
            sp.wait_ge(head_kept, 1)
            with nc.allow_non_contiguous_dma(reason="eight columns of decode tokens"):
                sp.dma_start(keep.mixed_dram[:, 4:8, SEQ:TOK], outT[:]).then_inc(head_stored, 16)
            sp.dma_start(g_ffn[:], row_broadcast(io["g_ffn"], D)).then_inc(consts, 16)
            sp.dma_start(keep.gate_raw, io["w_gate"][0].rearrange("(k p) n -> p k n", p=P)[:, :, 0:P])\
              .then_inc(keep.gate_in, 16)
            for i in range(NT):
                if i + 1 < NT:
                    load(i + 1)
                sp.wait_ge(x1_half, 2 * i + 2)
                sp.dma_start(keep.x_dram[i], x1[:, i % 2, :]).then_inc(stored[i % 2], 16)
            sp.wait_ge(stored[0], 16 * ((NT + 1) // 2))
            sp.wait_ge(stored[1], 16 * (NT // 2))

        @block.gpsimd
        def _(pool):
            step = Steps(pool, pool_step)
            for i in range(NT):
                pool.wait_ge(squared, i + 1)
                step(nc.gpsimd.tensor_tensor(sq[:, :, 0:2, :], sq[:, :, 0:2, :], sq[:, :, 2:4, :], ALU.add))
                nc.gpsimd.tensor_tensor(sq[:, :, 0, :], sq[:, :, 0, :], sq[:, :, 1, :], ALU.add).then_inc(chunks_added, 1)

        @block.tensor
        def _(pe):
            def sum_squares(i):
                pe.wait_ge(chunks_added, i + 1)
                if i >= 1:
                    pe.wait_ge(averaged, i)
                for a in range(2):
                    last = nc.tensor.matmul(SS[:, a, :], sq[:, a, 0, :], keep.ones[:], start=True, stop=True)
                last.then_inc(summed, 1)

            def turn(i):
                pe.wait_ge(normed, i + 1)
                for u in range(2):
                    if i >= 1:
                        pe.wait_ge(lo_done, 2 * i - 1 + u)
                    for j in range(4):
                        k = 4 * u + j
                        last = nc.tensor.transpose(T[:, u, j * P:(j + 1) * P], h2[:, k * P:(k + 1) * P], keep.ident[:])
                    last.then_inc(turned, 1)

            nc.tensor.matmul(L, keep.ones[:], keep.total[:].rearrange("p b h -> p (b h)"), start=True, stop=True)\
              .then_inc(sums_made, 1)
            for b in range(NB):
                for ck in range(2):
                    last = nc.tensor.matmul(F[:, b, ck, :], keep.ctx[:, b, ck * P:(ck + 1) * P], keep.fold[:],
                                            start=True, stop=True)
            last.then_inc(folded, 1)
            pe.wait_ge(fold_out, 1)
            pe.wait_ge(w_uv_in, 16)
            for h in range(NH):
                for ck in range(2):
                    last = nc.tensor.matmul(O[:, h * DV:(h + 1) * DV], ctxT[:, ck, h, :],
                                            keep.w_uv[:, ck, h * DV:(h + 1) * DV], start=(ck == 0), stop=(ck == 1))
            last.then_inc(head_out, 1)
            pe.wait_ge(head_normed, 1)
            for g in range(4):
                last = nc.tensor.transpose(OT[:, g * NB:(g + 1) * NB], out[:, g * P:(g + 1) * P],
                                           keep.ident[0:NB, 0:NB])
            last.then_inc(head_turned, 1)
            sum_squares(0)
            for i in range(NT):
                b = i % 2
                pe.wait_ge(m_lo_done, i + 1)
                for a in range(2):
                    if i >= 1:
                        pe.wait_ge(x1_half, 2 * i - 1 + a)
                    for k in range(4 * a, 4 * a + 4):
                        if i == 0:
                            pe.wait_ge(w_lo_done, k + 1)
                        for n, (h, w) in enumerate(((m_hi, w_hi), (m_hi, w_lo), (m_lo, w_hi))):
                            for g in range(2):
                                last = nc.tensor.matmul(OUT[:, a, g, :], h[:, b, k, :], w[:, k, g * 512:(g + 1) * 512],
                                                        start=(k == 4 * a and n == 0), stop=(k == 4 * a + 3 and n == 2))
                        if k == 6 and i + 1 < NT:
                            sum_squares(i + 1)
                    last.then_inc(half_done, 1)
                    if a == 0 and i >= 1:
                        turn(i - 1)
            turn(NT - 1)

        @block.scalar
        def _(act):
            step = Steps(act, act_step)

            def squares(i):
                act.wait_ge(m_in[i % 2], 16 * (i // 2 + 1))
                if i == PT:
                    act.wait_ge(pad_set, 2)
                if i >= 1:
                    act.wait_ge(summed, i)
                nc.scalar.activation(sq[:].rearrange("p a k t -> p (a k) t"), m[:, i % 2], ACT.Square).then_inc(squared, 1)
                if i >= 2:
                    act.wait_ge(half_done, 2 * i - 2)
                nc.scalar.activation(m_hi[:, i % 2], m[:, i % 2], ACT.Copy).then_inc(m_hi_done, 1)
                act.wait_ge(averaged, i + 1)
                step(nc.scalar.activation(log[:, 0:2], mean[:, 0:2], ACT.Ln))
                nc.scalar.activation(guess[:, 0:2], log[:, 0:2], ACT.Exp, scale=-0.5).then_inc(guessed, 1)

            def norm(i):
                act.wait_ge(x1_half, 2 * i + 2)
                if i >= 1:
                    act.wait_ge(lo_done, 2 * i)
                step(nc.scalar.activation(junk[:], x1[:, i % 2, :], ACT.Square, accum_out=ssx[:, i:i + 1]))
                step(nc.scalar.activation(log[:, 2:3], ssx[:, i:i + 1], ACT.Ln, bias=eps[:], scale=1.0 / D))
                nc.scalar.activation(guess[:, 2:3], log[:, 2:3], ACT.Exp, scale=-0.5).then_inc(x_guessed, 1)

            def hi(i):
                n = P if i < PT else NB
                for u in range(2):
                    act.wait_ge(turned, 2 * i + u + 1)
                    nc.scalar.activation(keep.h_hi[:, 4 * u:4 * u + 4, i * P:i * P + n],
                                         T[:, u, :].rearrange("p (c t) -> p c t", t=P)[:, :, 0:n],
                                         ACT.Copy).then_inc(hi_done, 1)

            act.wait_ge(folded, 1)
            nc.scalar.activation(ctxT[:].rearrange("p c h b -> p b c h"), F, ACT.Copy).then_inc(fold_out, 1)
            for k in range(DC):
                act.wait_ge(w_in[k % WB], 16 * (k // WB + 1))
                nc.scalar.activation(w_hi[:, k, :], w_raw[k % WB], ACT.Copy, scale=keep.g_out[:, k:k + 1])\
                  .then_inc(w_hi_done, 1)
                if k == 2:
                    squares(0)
            for i in range(NT):
                if i + 1 < NT:
                    squares(i + 1)
                norm(i)
                hi(i)

        @block.vector
        def _(dve):
            step = Steps(dve, dve_step)

            def split(i):
                dve.wait_ge(m_hi_done, i + 1)
                nc.vector.tensor_tensor(m_lo[:, i % 2], m[:, i % 2], m_hi[:, i % 2].bitcast(F32),
                                        ALU.subtract).then_inc(m_lo_done, 1)
                dve.wait_ge(summed, i + 1)
                nc.vector.tensor_scalar(mean[:, 0:2], SS[:, :, 0], 1.0 / PW, EPS, ALU.mult, ALU.add).then_inc(averaged, 1)
                if i == PT - 2:
                    dve.wait_ge(m_lo_done, i + 1)
                    nc.vector.memset(m[:, i % 2], 0.0).then_inc(pad_set, 1)
                dve.wait_ge(averaged, i + 1)
                dve.wait_ge(guessed, i + 1)
                step(newton_rsqrt(nc.vector, step, r_mix[:, i % 2], mean[:, 0:2], guess[:, 0:2], log[:, 0:2]))

            def add(i, halves):
                b = i % 2
                dve.wait_ge(x_in[b], 16 * (i // 2 + 1))
                for a in halves:
                    dve.wait_ge(half_done, 2 * i + a + 1)
                    if a == 0 and i >= 2:
                        dve.wait_ge(stored[b], 16 * (i // 2))
                    if a == 1:
                        dve.wait_ge(x1_half, 2 * i + 1)
                    nc.vector.scalar_tensor_tensor(out=x1[:, b, :], in0=OUT[:, a].rearrange("p g n -> p (g n)"),
                                                   scalar=r_mix[:, b, a:a + 1], in1=x[:, b, :] if a == 0 else x1[:, b, :],
                                                   op0=ALU.mult, op1=ALU.add).then_inc(x1_half, 1)
                if 1 in halves and i == PT - 2:
                    dve.wait_ge(x1_half, 2 * i + 2)
                    nc.vector.memset(x[:, b, :], 0.0).then_inc(pad_set, 1)

            def norm_x1(i):
                n = P if i < PT else NB
                dve.wait_ge(x_guessed, i + 1)
                step(nc.vector.tensor_scalar(mean[:, 2:3], ssx[:, i:i + 1], 1.0 / D, EPS, ALU.mult, ALU.add))
                step(newton_rsqrt(nc.vector, step, r_x1[:], mean[:, 2:3], guess[:, 2:3], log[:, 2:3]))
                nc.vector.scalar_tensor_tensor(out=h2[:], in0=x1[:, i % 2, :], scalar=r_x1[:], in1=g_ffn[:],
                                               op0=ALU.mult, op1=ALU.mult).then_inc(normed, 1)
                for u in range(2):
                    dve.wait_ge(hi_done, 2 * i + u + 1)
                    nc.vector.tensor_tensor(keep.h_lo[:, 4 * u:4 * u + 4, i * P:i * P + n],
                                            T[:, u, :].rearrange("p (c t) -> p c t", t=P)[:, :, 0:n],
                                            keep.h_hi[:, 4 * u:4 * u + 4, i * P:i * P + n].bitcast(F32),
                                            ALU.subtract).then_inc(lo_done, 1)

            nc.vector.memset(eps[:], EPS)
            dve.wait_ge(sums_made, 1)
            step(nc.vector.tensor_tensor(own[:], keep.own[:], L[0:NB].rearrange("p (b h) -> p b h", h=NH), ALU.mult))
            step(nc.vector.tensor_reduce(total[:], own[:].rearrange("p b h -> p h b"), AX.X, ALU.add))
            step(nc.vector.reciprocal(inv[:], total[:]))
            for k in range(DC):
                dve.wait_ge(w_in[k % WB], 16 * (k // WB + 1))
                dve.wait_ge(w_hi_done, k + 1)
                nc.vector.scalar_tensor_tensor(out=w_lo[:, k, :], in0=w_raw[k % WB], scalar=keep.g_out[:, k:k + 1],
                                               in1=w_hi[:, k, :].bitcast(F32), op0=ALU.mult,
                                               op1=ALU.subtract).then_inc(w_lo_done, 1)
                if k == 1:
                        dve.wait_ge(head_out, 1)
                        nc.vector.tensor_tensor(out.rearrange("p (h d) -> p h d", d=DV), O.rearrange("p (h d) -> p h d", d=DV),
                                                inv[:].unsqueeze(2).to_broadcast([NB, NH, DV]), ALU.mult).then_inc(head_normed, 1)
                        dve.wait_ge(head_turned, 1)
                        nc.vector.tensor_copy(outT[:].rearrange("p g b -> p (g b)"), OT).then_inc(head_kept, 1)
                if k == 2:
                    split(0)
            dve.wait_ge(consts, 16)
            dve.wait_ge(w_lo_done, DC)
            for i in range(NT):
                add(i, (0,))
                if i + 1 < NT:
                    split(i + 1)
                add(i, (1,))
                norm_x1(i)


def gate_and_up(nc, io, keep):
    with ExitStack() as stack:
        c = Ctx(nc, stack, "gu")
        raw = (keep.gate_raw, c.sb("up_raw", [P, DC, P])[:])
        w_hi = c.sb("w_hi", [P, 2, DC, P], F32R)
        w_lo = c.sb("w_lo", [P, 2, DC, P], F32R)
        room = c.sb("room", [P, 3, 1040])
        gate, acc, sig = room[:, 0, :], room[:, 1, 0:TOK], room[:, 2, 0:TOK]
        taps = c.sb("taps", [P, FC, 20])
        newc = keep.newc
        rows = keep.gT[0:20, FC - 3:FC, :].rearrange("p c t -> p (c t)")[:, 0:FF]
        GU = c.ps("GU", [P, 6, 512])
        T = c.ps("T", [P, FC, 20])
        raw_in = [keep.gate_in, c.sem("up_in")]
        hi_done = [c.sem("gate_hi"), c.sem("up_hi")]
        lo_done = [c.sem("gate_lo"), c.sem("up_lo")]
        ready = [c.sem("gate_ready"), c.sem("up_ready")]
        rows_in, turned, kept, padded = c.sem("rows_in"), c.sem("turned"), c.sem("kept"), c.sem("padded")
        gate_copied, convolved, exped, multiplied = (c.sem("gate_copied"), c.sem("convolved"), c.sem("exped"),
                                                     c.sem("multiplied"))
        dve_step = c.sem("dve_step")
        block = stack.enter_context(nc.Block())

        def chunks(eng, body):
            body(0, True, False)
            with eng.Fori(1, FC - 1) as f:
                body(f, False, False)
            body(FC - 1, False, True)

        @block.sync
        def _(sp):
            def load(kind, f):
                w = io[("w_gate", "w_up")[kind]][0].rearrange("(k p) n -> p k n", p=P)
                sp.dma_start(raw[kind], w[:, :, bass.ds(f * P, P)]).then_inc(raw_in[kind], 16)

            load(1, 0)
            sp.dma_start(rows[0:16, :], io["state_conv"][0].rearrange("b r c -> (b r) c")).then_inc(rows_in, 16)
            sp.dma_start(rows[16:19, :], io["conv_w"][0]).then_inc(rows_in, 16)
            sp.dma_start(rows[19:20, :], io["conv_b"]).then_inc(rows_in, 16)
            for par in range(2):
                sp.dma_start(keep.down_raw[:, par, :], io["w_down"][0, par * P:(par + 1) * P, :])\
                  .then_inc(keep.down_in[par], 16)
            with sp.Fori(1, FC) as f:
                for kind in range(2):
                    sp.wait_ge(lo_done[kind], f)
                    load(kind, f)

        @block.tensor
        def _(pe):
            def chunk(f, first, last):
                for kind in range(2):
                    pe.wait_ge(lo_done[kind], f + 1)
                    if not first:
                        pe.wait_ge((gate_copied, multiplied)[kind], f)
                    for k in range(DC):
                        for n, (w, h) in enumerate(((w_hi, keep.h_hi), (w_hi, keep.h_lo), (w_lo, keep.h_hi))):
                            for j in range(3):
                                ins = nc.tensor.matmul(GU[:, 3 * kind + j, 0:F3], w[:, kind, k, :],
                                                       h[:, k, j * F3:(j + 1) * F3], start=(k == 0 and n == 0),
                                                       stop=(k == DC - 1 and n == 2))
                    ins.then_inc(ready[kind], 1)
                    if first and kind == 0:
                        pe.wait_ge(rows_in, 48)
                        for n in range(FC):
                            ins = nc.tensor.transpose(T[:, n, :], rows[:, n * P:(n + 1) * P], keep.ident[0:20, 0:20])
                        ins.then_inc(turned, 1)

            chunks(pe, chunk)

        @block.scalar
        def _(act):
            def hi(kind, n_in):
                act.wait_ge(raw_in[kind], n_in)
                nc.scalar.activation(w_hi[:, kind], raw[kind], ACT.Copy).then_inc(hi_done[kind], 1)

            hi(0, 16)
            hi(1, 16)
            act.wait_ge(padded, 1)

            def chunk(f, first, last):
                act.wait_ge(ready[0], f + 1)
                if not first:
                    act.wait_ge(convolved, f)
                nc.scalar.activation(gate[:, 2:2 + TOK].rearrange("p (j t) -> p j t", j=3), GU[:, 0:3, 0:F3], ACT.Copy)\
                  .then_inc(gate_copied, 1)
                if not last:
                    hi(0, f * 16 + 32)
                act.wait_ge(convolved, f + 1)
                nc.scalar.activation(sig, acc, ACT.Exp, scale=-1.0).then_inc(exped, 1)
                if not last:
                    act.wait_ge(ready[1], f + 1)
                    hi(1, f * 16 + 32)

            chunks(act, chunk)

        @block.vector
        def _(dve):
            LINKS = 5
            nc.vector.memset(gate[:, 0:2], 0.0).then_inc(padded, 1)

            def lo(kind, f):
                dve.wait_ge(hi_done[kind], f + 1)
                nc.vector.tensor_tensor(w_lo[:, kind], raw[kind], w_hi[:, kind].bitcast(F32),
                                        ALU.subtract).then_inc(lo_done[kind], 1)

            lo(0, 0)
            lo(1, 0)
            dve.wait_ge(turned, 1)
            nc.vector.tensor_copy(taps[:], T[:]).then_inc(kept, 1)
            dve.wait_ge(kept, 1)

            def chunk(f, first, last):
                done = [0]

                def link(ins):
                    ins.then_inc(dve_step, 1)
                    done[0] += 1
                    dve.wait_ge(dve_step, f * LINKS + done[0])

                at = lambda a, z: taps[:, bass.ds(f, 1), a:z].rearrange("p o n -> p (o n)")
                state = taps[:, bass.ds(f, 1), 0:2 * NB].rearrange("p o (b r) -> p (o b) r", r=2)
                if not first:
                    dve.wait_ge(multiplied, f)
                dve.wait_ge(gate_copied, f + 1)
                link(nc.vector.tensor_scalar(acc, gate[:, 2:2 + TOK], at(18, 19), at(19, 20), ALU.mult, ALU.add))
                nc.vector.tensor_scalar(newc[:, bass.ds(f, 1), :].rearrange("p o n -> p (o n)"),
                                        gate[:, SEQ:SEQ + 2 + NB], 1.0, None, ALU.mult)
                for k in (1, 0):
                    nc.vector.scalar_tensor_tensor(out=acc[:, 0:SEQ], in0=gate[:, k:k + SEQ], scalar=at(16 + k, 17 + k),
                                                   in1=acc[:, 0:SEQ], op0=ALU.mult, op1=ALU.add)
                    ins = nc.vector.scalar_tensor_tensor(out=acc[:, SEQ:TOK], in0=state[:, :, k],
                                                         scalar=at(16 + k, 17 + k), in1=acc[:, SEQ:TOK],
                                                         op0=ALU.mult, op1=ALU.add)
                    if k == 1:
                        link(ins)
                    else:
                        ins.then_inc(convolved, 1)
                if not last:
                    lo(0, f + 1)
                dve.wait_ge(convolved, f + 1)
                dve.wait_ge(exped, f + 1)
                link(nc.vector.tensor_scalar(sig, sig, 1.0, None, ALU.add))
                link(nc.vector.reciprocal(sig, sig))
                link(nc.vector.tensor_tensor(acc, acc, sig, ALU.mult))
                dve.wait_ge(ready[1], f + 1)
                nc.vector.tensor_tensor(keep.gT[:, bass.ds(f, 1), :].rearrange("p o (j t) -> p (o j) t", j=3),
                                        acc.rearrange("p (j t) -> p j t", j=3), GU[:, 3:6, 0:F3], ALU.mult)\
                  .then_inc(multiplied, 1)
                if not last:
                    lo(1, f + 1)

            chunks(dve, chunk)


def down(nc, io, keep):
    with ExitStack() as stack:
        c = Ctx(nc, stack, "dn")
        TILE3 = 3
        PASSES = NT // TILE3
        raw = keep.down_raw
        w_hi = c.sb("w_hi", [P, 2, D], F32R)
        w_lo = c.sb("w_lo", [P, 2, D], F32R)
        g_hi = c.sb("g_hi", [P, 2, TILE3 * P], F32R)
        g_lo = c.sb("g_lo", [P, 2, TILE3 * P], F32R)
        y = c.sb("y", [P, TILE3, D])
        OUT = c.ps("OUT", [P, TILE3, 2, 512])
        T = c.ps("T", [P, 2, 512])
        w_in = keep.down_in
        x_in = [c.sem(f"x_in{n}") for n in range(TILE3)]
        stored = [c.sem(f"stored{n}") for n in range(TILE3)]
        w_hi_done, w_lo_done, g_hi_done, g_lo_done = (c.sem("w_hi_done"), c.sem("w_lo_done"), c.sem("g_hi_done"),
                                                      c.sem("g_lo_done"))
        used, added = c.sem("used"), c.sem("added")
        new_rows = y[0:2 + NB].rearrange("p t n -> p (t n)")[:, 0:FF]
        new_turned, new_kept, new_stored = c.sem("new_turned"), c.sem("new_kept"), c.sem("new_stored")
        NEW = [(a, min(a + 4, FC)) for a in range(0, FC, 4)]
        block = stack.enter_context(nc.Block())

        span = [(q * TILE3 * P, min(TOK, (q + 1) * TILE3 * P)) for q in range(PASSES)]
        HALVES = FC // 2

        def chunks(eng, q, body, between=None):
            for par in range(2):
                body(par, par, q * FC + par, q * HALVES)
                if par == 0 and between:
                    between()
            with eng.Fori(1, HALVES - 1) as j:
                for par in range(2):
                    body(par, j * 2 + par, j * 2 + (q * FC + par), j + q * HALVES)
            for par in range(2):
                body(par, FC - 2 + par, q * FC + FC - 2 + par, q * HALVES + HALVES - 1)

        def later(n):
            return not isinstance(n, int) or n >= 2

        @block.sync
        def _(sp):
            def load(par, f, n, r):
                if later(n):
                    sp.wait_ge(w_lo_done, n - 1)
                else:
                    return
                sp.dma_start(raw[:, par, :], io["w_down"][0].rearrange("(f p) n -> p f n", p=P)[:, bass.ds(f, 1), :]
                             .rearrange("p o n -> p (o n)")).then_inc(w_in[par], 16)

            for q in range(PASSES):
                chunks(sp, q, load)

        @block.gpsimd
        def _(pool):
            def load_x(q):
                if q == 0:
                    pool.wait_ge(new_kept, len(NEW))
                    pool.dma_start(io["new_conv_prompt"][0, 0], new_rows[0:2, :]).then_inc(new_stored, 16)
                    pool.dma_start(io["new_conv_sample"][0, :, 1, :], new_rows[2:2 + NB, :]).then_inc(new_stored, 16)
                    pool.wait_ge(new_stored, 32)
                for t in range(TILE3):
                    if q >= 1:
                        pool.wait_ge(stored[t], 16 * q)
                    pool.dma_start(y[:, t, :], keep.x_dram[q * TILE3 + t]).then_inc(x_in[t], 16)

            def store(q):
                for t in range(TILE3):
                    i = q * TILE3 + t
                    pool.wait_ge(added, i + 1)
                    if i < PT:
                        pool.dma_start(io["y_prompt"][0, i * P:(i + 1) * P, :], y[:, t, :]).then_inc(stored[t], 16)
                    else:
                        pool.dma_start(io["y_sample"][:, 0, :], y[0:NB, t, :]).then_inc(stored[t], 16)

            for q in range(PASSES):
                if q >= 1:
                    store(q - 1)
                load_x(q)
            store(PASSES - 1)
            for t in range(TILE3):
                pool.wait_ge(stored[t], 16 * PASSES)

        @block.tensor
        def _(pe):
            def turn_new(u):
                a, z = NEW[u]
                if u >= 2:
                    pe.wait_ge(new_kept, u - 1)
                for f in range(a, z):
                    last = nc.tensor.transpose(T[0:2 + NB, u % 2, (f - a) * P:(f - a + 1) * P], keep.newc[:, f, :],
                                               keep.ident[:])
                last.then_inc(new_turned, 1)

            for q in range(PASSES):
                def chunk(par, f, n, r, q=q):
                    if isinstance(n, int) and n < 2:
                        for u in ((0, 1, 2, 3), (4, 5))[n]:
                            turn_new(u)
                    pe.wait_ge(g_lo_done, n + 1)
                    for t in range(TILE3):
                        if q >= 1 and isinstance(f, int) and f == 0:
                            pe.wait_ge(added, (q - 1) * TILE3 + t + 1)
                        m = min(P, span[q][1] - span[q][0] - t * P)
                        for k, (g, w) in enumerate(((g_hi, w_hi), (g_hi, w_lo), (g_lo, w_hi))):
                            for z in range(2):
                                last = nc.tensor.matmul(OUT[0:m, t, z, :], g[:, par, t * P:t * P + m],
                                                        w[:, par, z * 512:(z + 1) * 512],
                                                        start=(isinstance(f, int) and f == 0 and k == 0),
                                                        stop=(isinstance(f, int) and f == FC - 1 and k == 2))
                    last.then_inc(used, 1)

                chunks(pe, q, chunk)

        @block.scalar
        def _(act):
            def keep_new(us):
                for u in us:
                    a, z = NEW[u]
                    act.wait_ge(new_turned, u + 1)
                    nc.scalar.activation(new_rows[:, a * P:z * P], T[0:2 + NB, u % 2, 0:(z - a) * P], ACT.Copy)\
                      .then_inc(new_kept, 1)

            for q in range(PASSES):
                def chunk(par, f, n, r, q=q):
                    a, z = span[q]
                    act.wait_ge(w_in[par], r * 16 + 16)
                    if later(n):
                        act.wait_ge(used, n - 1)
                    nc.scalar.activation(w_hi[:, par, :], raw[:, par, :], ACT.Copy).then_inc(w_hi_done, 1)
                    if isinstance(n, int) and n == 0:
                        keep_new((0, 1))
                    nc.scalar.activation(g_hi[:, par, 0:z - a],
                                         keep.gT[:, bass.ds(f, 1), a:z].rearrange("p o t -> p (o t)"), ACT.Copy)\
                      .then_inc(g_hi_done, 1)
                    if isinstance(n, int) and n < 2:
                        keep_new(((2, 3), (4, 5))[n])

                chunks(act, q, chunk)

        @block.vector
        def _(dve):
            def add(q):
                for t in range(TILE3):
                    i = q * TILE3 + t
                    m = P if i < PT else NB
                    dve.wait_ge(used, (q + 1) * FC)
                    dve.wait_ge(x_in[t], 16 * (q + 1))
                    nc.vector.tensor_tensor(y[0:m, t, :], y[0:m, t, :], OUT[0:m, t].rearrange("p z n -> p (z n)"),
                                            ALU.add).then_inc(added, 1)

            for q in range(PASSES):
                def chunk(par, f, n, r, q=q):
                    a, z = span[q]
                    dve.wait_ge(w_hi_done, n + 1)
                    nc.vector.tensor_tensor(w_lo[:, par, :], raw[:, par, :], w_hi[:, par, :].bitcast(F32),
                                            ALU.subtract).then_inc(w_lo_done, 1)
                    dve.wait_ge(g_hi_done, n + 1)
                    nc.vector.tensor_tensor(g_lo[:, par, 0:z - a],
                                            keep.gT[:, bass.ds(f, 1), a:z].rearrange("p o t -> p (o t)"),
                                            g_hi[:, par, 0:z - a].bitcast(F32), ALU.subtract).then_inc(g_lo_done, 1)

                chunks(dve, q, chunk, between=(lambda q=q: add(q - 1)) if q >= 1 else None)
            add(PASSES - 1)


class Keep:
    pass


def program(nc, io):
    with ExitStack() as stack:
        c = Ctx(nc, stack, "keep")
        keep = Keep()
        SEMAPHORES.taken = []
        keep.mixed_dram = nc.dram_tensor("mixed_scratch", (P, MIX // P, TOK), F32, kind="Internal").ap()
        keep.x_dram = nc.dram_tensor("x_scratch", (NT, P, D), F32, kind="Internal").ap()
        keep.ident = c.sb("ident", [P, P])
        keep.ones = c.sb("ones", [P, P])
        keep.sub_row = c.sb("sub_row", [P, 1])
        keep.fold = c.sb("fold", [P, NH])
        keep.own = c.sb("own", [NB, NB, NH])
        keep.g_out = c.sb("g_out", [P, DC])
        keep.total = c.sb("total", [P, NB, NH])
        keep.ctx = c.sb("ctx", [P, NB, RK])
        keep.q_s = keep.ctx[0:NB].rearrange("p b c -> p (b c)")[:, NH * DH:2 * NH * DH].rearrange("p (h d) -> p h d", h=NH)
        keep.w_uv = c.sb("w_uv", [P, RK // P, NH * DV])
        keep.gate_raw = keep.w_uv[:].rearrange("p c (a n) -> p (c a) n", n=P)
        keep.down_raw = keep.ctx[:].rearrange("p (t a) c -> p t (a c)", t=2)
        with ExitStack() as attention:
            c = Ctx(nc, attention, "attn")
            keep.w_uk = c.sb("w_uk", [P, RK // P, NH * DN])
            keep.s_own = c.sb("s_own", [NB, NH])
            keep.pages = c.sb("pages", [P, PAST // CHUNK * NB], I32)
            keep.index = c.sb("index", [P, PAST // CHUNK * NB], I32)
            keep.q_new = c.sb("q_new", [DH, NH, NB])
            keep.s_new = c.sb("s_new", [P, NB, NH])
            keep.q_pe = c.sb("q_pe", [P, NB, 4, NH])
            keep.qa_hi = c.sb("qa_hi", [P, 2, NB, NH], F32R)
            keep.qa_lo = c.sb("qa_lo", [P, 2, NB, NH], F32R)
            keep.ckv_s = c.sb("ckv_s", [P, RK])
            with ExitStack() as late:
                c = Ctx(nc, late, "late")
                keep.cos = c.sb("cos", [P, NT, HR])
                keep.sin = c.sb("sin", [P, NT, HR])
                keep.kpe = c.sb("kpe", [P, NT, DR])
                keep.room = c.sb("room", [P, NH * TOK])
                keep.qT = keep.room[0:DH, :].rearrange("p (h t) -> p h t", h=NH)
                with ExitStack() as mid:
                    c = Ctx(nc, mid, "mid")
                    keep.uT = c.sb("uT", [P, len(WINDOWS), HIST + SEQ])
                    keep.usT = c.sb("usT", [P, len(WINDOWS), NB, HIST + 1])
                    keep.cqT = c.sb("cqT", [P, RQ // P, NT * P])
                    keep.ckvT = c.sb("ckvT", [P, RK // P, NT * P])
                    project_in(nc, io, keep)
                    keep.kT = c.sb("kT", [DH, NH, SEQ])
                    keep.v = c.sb("v", [P, PT, NH * DV])
                    keep.mixT = c.sb("mixT", [P, MIX // P, TOK])
                    make_heads(nc, io, keep)
                    attend_prompt(nc, io, keep)
            SEMAPHORES.recycle(nc)
            with ExitStack() as decode:
                c = Ctx(nc, decode, "dec")
                keep.lat = c.sb("lat", [P, 2 * CHUNKS, 8 * RK])
                keep.kpe_slots = c.sb("kpe_slots", [P, 2 * CHUNKS, 8 * DR])
                keep.slot_in = [c.sem(f"slot_in{n}") for n in range(2 * CHUNKS)]
                attend_cache(nc, io, keep)
        SEMAPHORES.recycle(nc)
        with ExitStack() as mlp:
            c = Ctx(nc, mlp, "mlp")
            keep.h_hi = c.sb("h_hi", [P, DC, TOK], F32R)
            keep.h_lo = c.sb("h_lo", [P, DC, TOK], F32R)
            keep.newc = c.sb("newc", [P, FC, 2 + NB])
            keep.gate_in = c.sem("gate_in")
            keep.down_in = [c.sem(f"down_in{n}") for n in range(2)]
            merge(nc, io, keep)
            keep.gT = c.sb("gT", [P, FC, TOK])
            gate_and_up(nc, io, keep)
            down(nc, io, keep)


_OUTS = [
    ("y_prompt", (1, SEQ, D)), ("y_sample", (NB, 1, D)),
    ("new_ckv_prompt", (1, 1, SEQ, RK)), ("new_kpe_prompt", (1, 1, SEQ, DR)),
    ("new_pool_prompt", (1, 1, HIST, PW)), ("new_conv_prompt", (1, 1, 2, FF)),
    ("new_ckv_sample", (1, NB, 1, RK)), ("new_kpe_sample", (1, NB, 1, DR)),
    ("new_pool_sample", (1, NB, HIST, PW)), ("new_conv_sample", (1, NB, 2, FF)),
]


def constants():
    pos = np.zeros((NT, P), np.float32)
    pos[:PT] = np.arange(SEQ, dtype=np.float32).reshape(PT, P)
    pos[PT] = PAST
    inv = np.float32(ROPE_BASE) ** (-np.arange(0, DR, 2, dtype=np.float32) / np.float32(DR))
    ang = (pos[:, :, None] * inv[None, None, :]).astype(np.float32)
    t = np.arange(16)
    part = np.arange(P)
    return {
        "ident": np.eye(P, dtype=np.float32),
        "rope_cos": np.ascontiguousarray(np.cos(ang).astype(np.float32).transpose(1, 0, 2)),
        "rope_sin": np.ascontiguousarray(np.sin(ang).astype(np.float32).transpose(1, 0, 2)),
        "causal": np.where(part[None, :] <= part[:, None], 0.0, MASKED).astype(np.float32),
        "counts": np.broadcast_to(np.stack([1.0 / np.minimum(w, t + 1) for w in WINDOWS]).astype(np.float32),
                                  (P, 4, 16)).copy(),
        "fold": (part[:, None] % 32 == np.arange(NH)[None, :]).astype(np.float32),
        "own": np.broadcast_to((np.arange(NB)[:, None] == np.arange(NB)[None, :]).astype(np.float32)[:, :, None],
                               (NB, NB, NH)).copy(),
        "sub_row": (part % (PAGE // 8)).astype(np.float32).reshape(P, 1),
    }


def kernel(**inputs):
    import concourse.bacc as _bacc
    from concourse.bass_utils import run_bass_kernel_spmd as _run

    nc = _bacc.Bacc("TRN2", target_bir_lowering=False, num_devices=1)
    arrays, io = {}, {}
    for name, a in {**inputs, **constants()}.items():
        a = np.ascontiguousarray(a)
        arrays[f"in_{name}"] = a
        io[name] = nc.dram_tensor(f"in_{name}", a.shape, mybir.dt.from_np(a.dtype), kind="ExternalInput").ap()
    for name, shape in _OUTS:
        io[name] = nc.dram_tensor(f"out_{name}", shape, F32, kind="ExternalOutput").ap()
    program(nc, io)
    r = _run(nc, [arrays], core_ids=[0])
    return tuple(r.results[0][f"out_{name}"] for name, _ in _OUTS)
```
